# Optimizing a Trainium2 kernel written in Bass

```python
import jax, jax.numpy as jnp
from jax import lax
import numpy as np

D_MODEL = 1024
BATCH = 1
SEQ = 2048
DEPTH = 1

CHUNK = 64
ROPE_THETA = 10000.0
EPS = 1e-6
NEG_INF = -1e30

ATT_HEAD_DIM = 64
ATT_WIDTH = D_MODEL // 2
ATT_HEADS = ATT_WIDTH // ATT_HEAD_DIM
ATT_KV_HEADS = ATT_HEADS // 4
ATT_GROUP = ATT_HEADS // ATT_KV_HEADS
KV_WIDTH = ATT_KV_HEADS * ATT_HEAD_DIM
WINDOW = 128
WINDOW_CHUNKS = WINDOW // CHUNK
WIN_KEYS = WINDOW_CHUNKS * CHUNK

HGRN_WIDTH = D_MODEL - ATT_WIDTH
HGRN_EXPAND = 128
HGRN_HEADS = HGRN_WIDTH // HGRN_EXPAND
HGRN_HEAD_K = HGRN_EXPAND
HGRN_HEAD_V = HGRN_WIDTH // HGRN_HEADS

D_MIX = ATT_WIDTH + HGRN_WIDTH
_IN_SIZES = (ATT_WIDTH, KV_WIDTH, KV_WIDTH, ATT_WIDTH,
             HGRN_WIDTH, HGRN_WIDTH, HGRN_WIDTH, HGRN_WIDTH)
P_IN = int(sum(_IN_SIZES))
SPLIT_POINTS = tuple(int(v) for v in np.cumsum(_IN_SIZES)[:-1])

kernel_name = "hybrid_swa_sink_hgrn2_block"

def rmsnorm(x, w):
    xf = x.astype(jnp.float32)
    y = xf * lax.rsqrt(jnp.mean(xf * xf, axis=-1, keepdims=True) + EPS) * w.astype(jnp.float32)
    return y.astype(x.dtype)

def rope(x, pos):
    half = x.shape[-1] // 2
    inv = ROPE_THETA ** (-jnp.arange(half, dtype=jnp.float32) / half)
    ang = pos.astype(jnp.float32)[:, None] * inv[None, :]
    cos = jnp.cos(ang)[None, :, None, :]
    sin = jnp.sin(ang)[None, :, None, :]
    xf = x.astype(jnp.float32)
    x1, x2 = xf[..., :half], xf[..., half:]
    out = jnp.concatenate([x1 * cos - x2 * sin, x2 * cos + x1 * sin], axis=-1)
    return out.astype(x.dtype)

def _shift_chunks(t, j, nc):
    if j == 0:
        return t
    pad = ((0, 0), (j, 0)) + ((0, 0),) * (t.ndim - 2)
    return jnp.pad(t, pad)[:, :nc]

def sliding_window_sink_attention(q, k, v, sinks):
    B, S = q.shape[0], q.shape[1]
    nc = S // CHUNK
    qc = q.reshape(B, nc, CHUNK, ATT_KV_HEADS, ATT_GROUP, ATT_HEAD_DIM)
    kc = k.reshape(B, nc, CHUNK, ATT_KV_HEADS, ATT_HEAD_DIM)
    vc = v.reshape(B, nc, CHUNK, ATT_KV_HEADS, ATT_HEAD_DIM)
    order = range(WINDOW_CHUNKS - 1, -1, -1)
    kb = jnp.concatenate([_shift_chunks(kc, j, nc) for j in order], axis=2)
    vb = jnp.concatenate([_shift_chunks(vc, j, nc) for j in order], axis=2)
    src_chunk = (jnp.arange(nc)[:, None] - (WINDOW_CHUNKS - 1)
                 + jnp.arange(WIN_KEYS)[None, :] // CHUNK)
    valid = src_chunk >= 0
    scale = ATT_HEAD_DIM ** -0.5
    s = jnp.einsum('bclhgd,bcmhd->bchglm', qc, kb).astype(jnp.float32) * scale
    s = jnp.where(valid[None, :, None, None, None, :], s, NEG_INF)
    sink = sinks.astype(jnp.float32).reshape(1, 1, ATT_KV_HEADS, ATT_GROUP, 1, 1)
    sink = jnp.broadcast_to(sink, s.shape[:-1] + (1,))
    p = jax.nn.softmax(jnp.concatenate([s, sink], axis=-1), axis=-1)[..., :-1]
    o = jnp.einsum('bchglm,bcmhd->bclhgd', p.astype(v.dtype), vb)
    return o.reshape(B, S, ATT_WIDTH)

def hgrn2_chunkwise(q, f_logit, i, lb):
    B, S = q.shape[0], q.shape[1]
    nc = S // CHUNK
    f32 = jnp.float32
    f = lb[None, None] + (1.0 - lb[None, None]) * jax.nn.sigmoid(f_logit.astype(f32))
    log_f = jnp.log(f)
    kk = 1.0 - f
    qf = q.astype(f32).reshape(B, nc, CHUNK, HGRN_HEADS, HGRN_HEAD_K)
    kf = kk.reshape(B, nc, CHUNK, HGRN_HEADS, HGRN_HEAD_K)
    vf = i.astype(f32).reshape(B, nc, CHUNK, HGRN_HEADS, HGRN_HEAD_V)
    G = jnp.cumsum(log_f.reshape(B, nc, CHUNK, HGRN_HEADS, HGRN_HEAD_K), axis=2)
    q_dec = qf * jnp.exp(G)
    k_dec = kf * jnp.exp(-G)
    causal = jnp.tril(jnp.ones((CHUNK, CHUNK), dtype=bool))
    A = jnp.einsum('bclhk,bcmhk->bchlm', q_dec, k_dec)
    A = jnp.where(causal[None, None, None], A, 0.0)
    o_intra = jnp.einsum('bchlm,bcmhv->bclhv', A, vf)
    G_last = G[:, :, -1]
    k_to_end = kf * jnp.exp(G_last[:, :, None] - G)
    U = jnp.einsum('bclhk,bclhv->bchkv', k_to_end, vf)
    decay = jnp.exp(G_last)

    def step(state, inp):
        d, u = inp
        return d[..., None] * state + u, state

    S0 = jnp.zeros((B, HGRN_HEADS, HGRN_HEAD_K, HGRN_HEAD_V), f32)
    _, S_prev = lax.scan(step, S0, (jnp.moveaxis(decay, 1, 0), jnp.moveaxis(U, 1, 0)))
    S_prev = jnp.moveaxis(S_prev, 0, 1)
    o_inter = jnp.einsum('bclhk,bchkv->bclhv', q_dec, S_prev)
    o = (o_intra + o_inter).reshape(B, S, HGRN_HEADS, HGRN_HEAD_V)
    return o.astype(q.dtype)

def setup_inputs(seed: int = 0) -> dict:
    key = jax.random.key(seed)
    ks = jax.random.split(key, 8)
    x = jax.random.normal(ks[0], (BATCH, SEQ, D_MODEL), jnp.float32)
    w_norm_pre = 1.0 + 0.01 * jax.random.normal(ks[1], (DEPTH, D_MODEL), jnp.float32)
    w_in = jax.random.normal(ks[2], (DEPTH, D_MODEL, P_IN), jnp.float32) * D_MODEL ** -0.5
    attn_sinks = 0.5 * jax.random.normal(ks[3], (DEPTH, ATT_HEADS), jnp.float32)
    hgrn_lb = 0.1 * jax.random.normal(ks[4], (DEPTH + 1, HGRN_WIDTH), jnp.float32)
    hgrn_norm = 1.0 + 0.01 * jax.random.normal(ks[5], (DEPTH, HGRN_HEAD_V), jnp.float32)
    w_out = jax.random.normal(ks[6], (DEPTH, D_MIX, D_MODEL), jnp.float32) * D_MIX ** -0.5
    w_norm_post = 1.0 + 0.01 * jax.random.normal(ks[7], (DEPTH, D_MODEL), jnp.float32)
    return {"x": x, "w_norm_pre": w_norm_pre, "w_in": w_in, "attn_sinks": attn_sinks,
            "hgrn_lb": hgrn_lb, "hgrn_norm": hgrn_norm, "w_out": w_out,
            "w_norm_post": w_norm_post}

def reference(x, w_norm_pre, w_in, attn_sinks, hgrn_lb, hgrn_norm, w_out, w_norm_post):
    B, S = x.shape[0], x.shape[1]
    pos = jnp.arange(S, dtype=jnp.int32)
    lb_all = jnp.cumsum(jax.nn.softmax(hgrn_lb.astype(jnp.float32), axis=0), axis=0)
    for l in range(DEPTH):
        h = rmsnorm(x, w_norm_pre[l])
        proj = h @ w_in[l]
        q_a, k_a, v_a, z_a, q_r, f_r, i_r, z_r = jnp.split(proj, SPLIT_POINTS, axis=-1)
        q_a = rope(q_a.reshape(B, S, ATT_HEADS, ATT_HEAD_DIM), pos)
        k_a = rope(k_a.reshape(B, S, ATT_KV_HEADS, ATT_HEAD_DIM), pos)
        v_a = v_a.reshape(B, S, ATT_KV_HEADS, ATT_HEAD_DIM)
        o_a = sliding_window_sink_attention(q_a, k_a, v_a, attn_sinks[l]) * jax.nn.silu(z_a)
        lb = lb_all[l].reshape(HGRN_HEADS, HGRN_HEAD_K)
        o_r = hgrn2_chunkwise(q_r.reshape(B, S, HGRN_HEADS, HGRN_HEAD_K),
                              f_r.reshape(B, S, HGRN_HEADS, HGRN_HEAD_K),
                              i_r.reshape(B, S, HGRN_HEADS, HGRN_HEAD_V), lb)
        o_r = rmsnorm(o_r, hgrn_norm[l]).reshape(B, S, HGRN_WIDTH) * jax.nn.silu(z_r)
        y = jnp.concatenate([o_a, o_r], axis=-1) @ w_out[l]
        x = x + rmsnorm(y, w_norm_post[l])
    return x


_drawn_inputs = setup_inputs


def setup_inputs(seed=0):
    import zlib

    import numpy as np

    out = dict(_drawn_inputs(seed))
    spreads = {}
    factors = {'w_norm_pre': 3.397, 'attn_sinks': 64.0, 'hgrn_norm': 37.797, 'w_norm_post': 46.243}
    for name, (base, spread) in spreads.items():
        noise = np.random.default_rng([zlib.crc32(name.encode()), seed]).standard_normal(out[name].shape)
        drawn = base * np.exp(spread * noise) if base else spread * noise
        out[name] = __import__('jax').numpy.asarray(drawn.astype(out[name].dtype))
    for name, factor in factors.items():
        out[name] = (out[name] * factor).astype(out[name].dtype)
    return out
```

```python
import math
from contextlib import ExitStack

import numpy as np
import concourse.bass as bass
from concourse import mybir

FP32 = mybir.dt.float32
FP32R = mybir.dt.float32r
INT32 = mybir.dt.int32
ALU = mybir.AluOpType
ACT = mybir.ActivationFunctionType
AX = mybir.AxisListType

P = 128
SEQ, D_MODEL = 2048, 1024
N = 512
TILES = SEQ // N
KT = D_MODEL // P
CHUNK = 64
CHUNKS = N // CHUNK
PAIRS = N // P
HEADS = 4
QT = 4
EPS = 1e-6
NEG_INF = -1e30
SCALE = 0.125
ROPE_THETA = 10000.0

K_TILE, V_TILE = 0, 1
Q0, Z0 = 2, 2 + QT
H0 = Z0 + QT
OUT0 = H0 + 4 * HEADS
WT = OUT0 + KT
ROPE_TILES = [K_TILE] + [Q0 + j for j in range(QT)]
SLOTS = 4
SLOT_USES = [len(range(s, WT, SLOTS)) for s in range(SLOTS)]

SCORES0 = Z0 + 3
PAIR0 = H0 + 3
XSQ0 = PAIR0 + 5
XSUM = XSQ0 + KT
H_NEW0 = XSUM + 1


def forget(h):
    return H0 + 4 * h


def query(h):
    return H0 + 4 * h + 1


def value(h):
    return H0 + 4 * h + 2


def gate(h):
    return H0 + 4 * h + 3


def before(w):
    if w >= SLOTS:
        return w - SLOTS
    return max(v for v in range(WT) if v % SLOTS == w % SLOTS) - WT


class Count:

    def __init__(self, sem, per_tile):
        self.sem, self.per_tile = sem, per_tile

    def start(self, engine):
        engine.sem_inc(self.sem, self.per_tile)

    def after(self, tile, i):
        assert -self.per_tile <= i < self.per_tile
        return tile * self.per_tile + (self.per_tile + i + 1)


def hybrid_block(nc, x, weights, cos, sin, vectors, squares, out):
    ctx = ExitStack()
    with ctx:
        def sb(name, shape, dt=FP32):
            return ctx.enter_context(nc.sbuf_tensor(name, [P] + shape, dt))

        def sem(name):
            return ctx.enter_context(nc.semaphore(name))

        x_in = sb("x_in", [KT, N])
        h_hi, h_lo = sb("h_hi", [KT, N], FP32R), sb("h_lo", [KT, N], FP32R)
        mix_hi, mix_lo = sb("mix_hi", [KT, N], FP32R), sb("mix_lo", [KT, N], FP32R)
        w_raw = sb("w_raw", [SLOTS, KT, P])
        w_hi, w_lo = sb("w_hi", [SLOTS, KT, P], FP32R), sb("w_lo", [SLOTS, KT, P], FP32R)
        q_gate = sb("q_gate", [2 * QT, N])
        queries = q_gate[:, 0:QT, :].rearrange("p q n -> p (q n)").rearrange(
            "p (h c j n) -> p h c j n", h=2, c=CHUNKS, j=2)
        k_t = sb("k_t", [2, CHUNK + N])
        v_t = sb("v_t", [CHUNK + N])
        cos_t, sin_t = sb("cos_t", [N]), sb("sin_t", [N])
        f_a, f_b, f_c, f_d = (sb(f"f_{c}", [N]) for c in "abcd")
        g_a = sb("g_a", [N])
        q_dec, k_dec, k_end = sb("q_dec", [N]), sb("k_dec", [N]), sb("k_end", [N])
        v_r, z_r, h_mix = sb("v_r", [N]), sb("z_r", [N]), sb("h_mix", [N])
        probs = sb("probs", [2, 4, P])
        probs_t = sb("probs_t", [N])
        v_tok = sb("v_tok", [P])
        k_tok = sb("k_tok", [2, P])
        v_rtok = sb("v_rtok", [P])
        a_t = sb("a_t", [P])
        o_tok = sb("o_tok", [P])
        carry = sb("carry", [HEADS, P])
        ring = sb("ring", [4, P])
        x_sq, x_acc = sb("x_sq", [N]), sb("x_acc", [N])
        reset = sb("reset", [N])
        ones = sb("ones", [P])
        sq_in = sb("sq_in", [2, P])
        ident = sq_in[:, 0, :]
        causal = sq_in[:, 1, :].bitcast(INT32)
        first_mask = sb("first_mask", [P])
        vec = sb("vec", [2 * KT + 1 + 2 * HEADS + 4])
        w_pre, w_post = vec[:, 0:KT], vec[:, KT:2 * KT]
        w_head = vec[:, 2 * KT:2 * KT + 1]
        lb_in = vec[:, 2 * KT + 1:2 * KT + 1 + 2 * HEADS]
        sink_in = vec[:, 2 * KT + 1 + 2 * HEADS:]
        lb, lb_rest = sb("lb", [HEADS]), sb("lb_rest", [HEADS])
        lb_e = sb("lb_e", [2 * HEADS])
        lb_m = sb("lb_m", [HEADS])
        sink8 = sb("sink8", [4])
        g_last = sb("g_last", [CHUNKS])
        decay = sb("decay", [2, CHUNKS])
        top, s_max, s_sum, s_inv = (sb(n, [4]) for n in ("top", "s_max", "s_sum", "s_inv"))
        sink_d = sb("sink_d", [4])
        o_sq = sb("o_sq", [1])
        eps = sb("eps", [1])

        bank = [ctx.enter_context(nc.psum_tensor(f"bank{i}", [P, N], FP32)) for i in range(8)]
        score_b, probs_b, att_b, tok_b, pair_b = bank[3:]

        def acc(w):
            if w in (OUT0 + 3, WT - 1):
                return score_b
            order = [i for i in range(WT) if i not in (OUT0 + 3, WT - 1)]
            return bank[order.index(w) % 3]

        def acc_before(w):
            for v in range(w - 1, w - WT - 1, -1):
                if acc(v % WT) is acc(w):
                    return v

        x_loaded, tables_loaded = sem("x_loaded"), sem("tables_loaded")
        w_loaded = [sem(f"w_loaded{i}") for i in range(SLOTS)]
        swapped = [sem(f"swapped{i}") for i in range(2)]
        res_loaded = sem("res_loaded")
        stored = [sem(f"stored{i}") for i in range(2)]

        def count(name, per_tile):
            return Count(sem(name), per_tile)

        tile_done = count("tile_done", WT)
        x_summed, y_summed = count("x_summed", 1), count("y_summed", 1)
        scored, turned, weighed = (count(n, CHUNKS) for n in ("scored", "turned", "weighed"))
        G = HEADS * PAIRS
        to_tok, a_u, o_done, o_turned = (count(n, G) for n in ("to_tok", "a_u", "o_done", "o_turned"))
        hi_split = count("hi_split", WT)
        gate_ln, gate_sig = (count(n, QT + HEADS) for n in ("gate_ln", "gate_sig"))
        f_ln, f_sig, f_log, f_exp, f_end = (count(n, HEADS) for n in ("f_ln", "f_sig", "f_log", "f_exp", "f_end"))
        p_exp, p_turned = count("p_exp", CHUNKS), count("p_turned", CHUNKS)
        kv_ready, o_normed = count("kv_ready", G), count("o_normed", G)
        mixa_hi, mixh_hi = count("mixa_hi", QT), count("mixh_hi", HEADS)
        x_squared, h_hi_done = count("x_squared", KT), count("h_hi_done", KT)
        y_squared, x_rstd, y_rstd = count("y_squared", KT), count("x_rstd", 1), count("y_rstd", 1)
        act_step = count("act_step", 2 * (QT + HEADS) + 2 * HEADS + 3 * HEADS * PAIRS + 2)
        tile_read = count("tile_read", WT)
        roped = count("roped", len(ROPE_TILES))
        gate_arg = count("gate_arg", QT + HEADS)
        f_gate, f_scan, f_rel = (count(n, HEADS) for n in ("f_gate", "f_scan", "f_rel"))
        a_masked, state_b, state_c, mixed = (count(n, G) for n in ("a_masked", "state_b", "state_c", "mixed"))
        head_mixed = count("head_mixed", HEADS)
        m_sub, p_inv, gated = (count(n, CHUNKS) for n in ("m_sub", "p_inv", "gated"))
        h_scaled, h_lo_done = count("h_scaled", KT), count("h_lo_done", KT)
        y_scaled, y_even = count("y_scaled", KT), count("y_even", KT // 2)
        dve_step = count("dve_step", len(ROPE_TILES) + CHUNKS * 4 + 1 + HEADS * 2)
        dve_setup, lb_step = sem("dve_setup"), sem("lb_step")
        act_setup = sem("act_setup")
        lo_split = count("lo_split", WT)
        k_dec_done, k_end_done = count("k_dec_done", HEADS), count("k_end_done", HEADS)
        p_normed = count("p_normed", CHUNKS)
        mixa_lo, mixh_lo = count("mixa_lo", QT), count("mixh_lo", HEADS)
        x_added, y_added = count("x_added", KT - 1), count("y_added", KT - 2)
        y_odd = count("y_odd", KT // 2)

        def loaded(sems, uses, tile, i, n=1):
            return (sems, tile * (16 * n * uses) + 16 * n * (i + 1))

        def wait_weights(engine, tile, w):
            engine.wait_ge(*loaded(w_loaded[w % SLOTS], SLOT_USES[w % SLOTS], tile, w // SLOTS))

        def chunk(c, n=1):
            return slice(c * CHUNK, (c + n) * CHUNK)

        def pair(p):
            return slice(p * P, (p + 1) * P)

        block = ctx.enter_context(nc.Block())

        @block.sync
        def _(sp):
            def load_x(tile, row):
                sp.wait_ge(h_lo_done.sem, h_lo_done.after(tile, -1))
                sp.wait_ge(y_even.sem, y_even.after(tile - 1, -1))
                sp.wait_ge(y_odd.sem, y_odd.after(tile - 1, -1))
                sp.dma_start(x_in[:, :, :], x[bass.ts(row, P), :].rearrange("p (k n) -> p k n", k=KT)).then_inc(x_loaded, 16)

            def load_weights(tile, w):
                sp.wait_ge(lo_split.sem, lo_split.after(tile, before(w)))
                sp.dma_start(w_raw[:, w % SLOTS, :, :],
                             weights[w * P:(w + 1) * P, :].rearrange("p (k m) -> p k m", k=KT)).then_inc(w_loaded[w % SLOTS], 16)

            sp.dma_start(x_in[:, :, :], x[0:P, :].rearrange("p (k n) -> p k n", k=KT)).then_inc(x_loaded, 16)
            with sp.Fori(0, TILES) as t:
                for w in range(WT):
                    load_weights(t, w)
                    if w == 0:
                        sp.wait_ge(roped.sem, roped.after(t, -1))
                        sp.dma_start(cos_t[:, :], cos[bass.ts(t, P), :]).then_inc(tables_loaded, 16)
                        sp.dma_start(sin_t[:, :], sin[bass.ts(t, P), :]).then_inc(tables_loaded, 16)
                    if w == H0:
                        load_x(t + 1, (t + 1) % TILES)
                sp.wait_ge(h_lo_done.sem, h_lo_done.after(t + 1, KT - 1))
                sp.dma_start(x_in[:, :, :], x[bass.ts(t, P), :].rearrange("p (k n) -> p k n", k=KT)).then_inc(res_loaded, 16)
            for w in range(2):
                load_weights(TILES, w)
            for w in range(2):
                wait_weights(sp, TILES, w)
            for s in stored:
                sp.wait_ge(s, 16 * (TILES + 1))

        @block.tensor
        def _(pe):
            for c in (tile_done, x_summed, y_summed, scored, turned, weighed, to_tok, a_u, o_done, o_turned):
                c.start(pe)

            def sum_x(tile):
                pe.wait_ge(x_added.sem, x_added.after(tile, KT - 2))
                pe.matmul(probs_b[:, :], ones[:, :], x_acc[:, :], start=True, stop=True).then_inc(x_summed.sem, 1)

            def products(w, m, last):
                k, part = m // 3, m % 3
                s = w % SLOTS
                hi, lo = (h_hi, h_lo) if w < OUT0 else (mix_hi, mix_lo)
                stationary, moving = ((w_hi, hi), (w_lo, hi), (w_hi, lo))[part]
                mm = pe.matmul(acc(w)[:, :], stationary[:, s, k, :], moving[:, k, :],
                               start=(m == 0), stop=(m == 3 * KT - 1), skip_group_check=True)
                if last:
                    mm.then_inc(tile_done.sem, 1)

            def scores(t, c):
                if c == 0:
                    pe.wait_ge(roped.sem, roped.after(t, QT))
                    pe.wait_ge(tile_read.sem, tile_read.after(t, -1))
                else:
                    pe.wait_ge(m_sub.sem, m_sub.after(t, c - 1))
                for b in range(4):
                    g, hp = b // 2, b % 2
                    mm = pe.matmul(score_b[:, pair(b)], queries[:, hp, c, :, :].rearrange("p j n -> p (j n)"),
                                   k_t[:, g, chunk(c, 2)], start=True, stop=True)
                mm.then_inc(scored.sem, 1)

            def turn(t, c):
                pe.wait_ge(gated.sem, gated.after(t, c - 1))
                pe.transpose(att_b[:, 2 * P:3 * P], v_t[:, chunk(c, 2)], ident)
                pe.wait_ge(p_normed.sem, p_normed.after(t, c))
                for b in range(4):
                    mm = pe.transpose(probs_b[:, pair(b)], probs[:, c % 2, b, :], ident)
                mm.then_inc(turned.sem, 1)

            def weigh(t, c):
                pe.wait_ge(p_turned.sem, p_turned.after(t, c))
                for g in range(2):
                    mm = pe.matmul(att_b[64 * g:64 * g + 64, 0:2 * P], v_tok[:, 64 * g:64 * g + 64],
                                   probs_t[:, 2 * P * g:2 * P * (g + 1)], start=True, stop=True)
                mm.then_inc(weighed.sem, 1)

            def pair_to_tok(t, g):
                h, p = divmod(g, PAIRS)
                if p == 0:
                    pe.wait_ge(k_end_done.sem, k_end_done.after(t, h))
                    pe.wait_ge(tile_read.sem, tile_read.after(t, value(h)))
                pe.transpose(tok_b[:, 0:P], k_end[:, pair(p)], ident)
                pe.transpose(tok_b[:, P:2 * P], v_r[:, pair(p)], ident).then_inc(to_tok.sem, 1)

            def pair_products(t, g):
                h, p = divmod(g, PAIRS)
                if p == 0:
                    pe.wait_ge(k_dec_done.sem, k_dec_done.after(t, h))
                pe.wait_ge(mixed.sem, mixed.after(t, g - 1))
                pe.wait_ge(kv_ready.sem, kv_ready.after(t, g))
                pe.matmul(pair_b[:, 0:P], k_dec[:, pair(p)], q_dec[:, pair(p)], start=True, stop=True)
                pe.matmul(pair_b[:, P:2 * P], k_tok[:, 0, :], v_rtok[:, :], start=True, stop=True)
                pe.matmul(pair_b[:, 2 * P:3 * P], k_tok[:, 1, :], v_rtok[:, :], start=True, stop=True).then_inc(a_u.sem, 1)

            def states(g):
                h, p = divmod(g, PAIRS)
                a = carry[:, h, :] if p == 0 else ring[:, (2 * p + 3) % 4, :]
                c = carry[:, h, :] if p == PAIRS - 1 else ring[:, (2 * p + 1) % 4, :]
                return a, ring[:, (2 * p) % 4, :], c

            def pair_out(t, g):
                h, p = divmod(g, PAIRS)
                state_a, state_m, _ = states(g)
                o = tok_b[:, 2 * P:3 * P]
                pe.wait_ge(a_masked.sem, a_masked.after(t, g))
                pe.matmul(o, a_t[:, :], v_rtok[:, :], start=True, stop=False, skip_group_check=True)
                pe.matmul(o[0:64, :], q_dec[:, chunk(2 * p)], state_a, start=False, stop=False, skip_group_check=True)
                pe.matmul(o[64:128, :], q_dec[:, chunk(2 * p + 1)], state_m, start=False, stop=True,
                          skip_group_check=True).then_inc(o_done.sem, 1)

            def pair_turn(t, g):
                pe.wait_ge(state_c.sem, state_c.after(t, g))
                pe.wait_ge(o_normed.sem, o_normed.after(t, g))
                pe.transpose(pair_b[:, 3 * P:4 * P], o_tok[:, :], ident).then_inc(o_turned.sem, 1)

            def between(t, w, m):
                g = w - PAIR0
                c = w - SCORES0
                if m == 0 and 1 <= g <= G:
                    pair_out(t, g - 1)
                if m == 4:
                    if 0 <= c < CHUNKS:
                        scores(t, c)
                    if 1 <= c <= CHUNKS:
                        turn(t, c - 1)
                    if w == XSUM:
                        sum_x(t + 1)
                if m == 8:
                    if 1 <= g <= G:
                        pair_turn(t, g - 1)
                    if 0 <= g < G:
                        pair_to_tok(t, g)
                if m == 12 and 1 <= c <= CHUNKS:
                    weigh(t, c - 1)
                if m == 16 and 0 <= g < G:
                    pair_products(t, g)

            pe.wait_ge(stored[1], 16)
            pe.wait_ge(dve_setup, 1)
            sum_x(0)
            with pe.Fori(0, TILES) as t:
                pe.wait_ge(h_lo_done.sem, h_lo_done.after(t, KT - 1))
                for w in range(OUT0):
                    pe.wait_ge(lo_split.sem, lo_split.after(t, w))
                    pe.wait_ge(tile_read.sem, tile_read.after(t, acc_before(w)))
                    for m in range(3 * KT):
                        between(t, w, m)
                        products(w, m, m == 3 * KT - 1)
                pe.wait_ge(mixa_lo.sem, mixa_lo.after(t, QT - 1))
                pe.wait_ge(mixh_lo.sem, mixh_lo.after(t, HEADS - 2))
                for w in range(OUT0, OUT0 + 4):
                    pe.wait_ge(lo_split.sem, lo_split.after(t, w))
                    pe.wait_ge(tile_read.sem, tile_read.after(t, acc_before(w)))
                    for m in range(3 * (KT - 1)):
                        between(t, w, m)
                        products(w, m, False)
                pe.wait_ge(mixh_lo.sem, mixh_lo.after(t, HEADS - 1))
                for w in range(OUT0, OUT0 + 4):
                    for m in range(3 * (KT - 1), 3 * KT):
                        products(w, m, m == 3 * KT - 1)
                for w in range(OUT0 + 4, WT):
                    pe.wait_ge(lo_split.sem, lo_split.after(t, w))
                    pe.wait_ge(tile_read.sem, tile_read.after(t, acc_before(w)))
                    for m in range(3 * KT):
                        products(w, m, m == 3 * KT - 1)
                pe.wait_ge(y_added.sem, y_added.after(t, KT - 3))
                pe.matmul(att_b[:, :], ones[:, :], f_c[:, :], start=True, stop=False)
                pe.wait_ge(y_squared.sem, y_squared.after(t, KT - 1))
                pe.matmul(att_b[:, :], ones[:, :], f_d[:, :], start=False, stop=True).then_inc(y_summed.sem, 1)

        @block.scalar
        def _(act):
            for c in (hi_split, gate_ln, gate_sig, f_ln, f_sig, f_log, f_exp, f_end, p_exp, p_turned, kv_ready,
                      o_normed, mixa_hi, mixh_hi, x_squared, h_hi_done, y_squared, x_rstd, y_rstd, act_step):
                c.start(act)
            act.preload_act_table_set("natural_log_exp_and_others")
            links = [0]

            def then(tile, instruction):
                instruction.then_inc(act_step.sem, 1)
                act.wait_ge(act_step.sem, act_step.after(tile, links[0]))
                links[0] += 1

            def split_hi(tile, w):
                act.wait_ge(tile_done.sem, tile_done.after(tile, before(w)))
                wait_weights(act, tile, w)
                act.activation(w_hi[:, w % SLOTS, :, :], w_raw[:, w % SLOTS, :, :], ACT.Copy).then_inc(hi_split.sem, 1)

            def log1p_exp(tile, src, dst):
                then(tile, act.activation(dst, src, ACT.Abs))
                then(tile, act.activation(dst, dst, ACT.Exp, scale=-1.0))
                return act.activation(dst, dst, ACT.Ln, bias=1.0)

            def gate_first(t, w, i):
                act.wait_ge(tile_done.sem, tile_done.after(t, w))
                if i == QT:
                    act.wait_ge(tile_read.sem, tile_read.after(t, Z0 + QT - 1))
                elif i:
                    act.wait_ge(tile_read.sem, tile_read.after(t, Z0 + i - 1 if i < QT else gate(i - QT - 1)))
                log1p_exp(t, acc(w)[:, :], g_a[:, :]).then_inc(gate_ln.sem, 1)

            def gate_second(t, i):
                act.wait_ge(gate_arg.sem, gate_arg.after(t, i))
                act.activation(g_a[:, :], g_a[:, :], ACT.Exp).then_inc(gate_sig.sem, 1)

            def rstd(tile, src, dst, width):
                then(tile, act.activation(dst, src, ACT.Ln, scale=1.0 / width, bias=eps[:, :]))
                return act.activation(dst, dst, ACT.Exp, scale=-0.5)

            def square_x(tile, k):
                if k == 0:
                    act.wait_ge(x_loaded, tile * 16 + 16)
                else:
                    act.wait_ge(x_added.sem, x_added.after(tile, k - 2))
                dst = x_acc if k == 0 else x_sq
                act.activation(dst[:, :], x_in[:, k, :], ACT.Square).then_inc(x_squared.sem, 1)

            def round_h(tile, k):
                act.wait_ge(h_scaled.sem, h_scaled.after(tile, k))
                act.activation(h_hi[:, k, :], x_in[:, k, :], ACT.Copy).then_inc(h_hi_done.sem, 1)

            def square_y(t, n):
                dst = f_c if n == 0 else (g_a, f_d)[n % 2]
                act.wait_ge(tile_done.sem, tile_done.after(t, OUT0 + n))
                if n >= 3:
                    act.wait_ge(y_added.sem, y_added.after(t, n - 3))
                act.activation(dst[:, :], acc(OUT0 + n)[:, :], ACT.Square).then_inc(y_squared.sem, 1)

            act.wait_ge(dve_setup, 2)
            act.activation(lb_e[:, :], lb_e[:, :], ACT.Exp).then_inc(act_setup, 1)
            for k in range(KT):
                square_x(0, k)
            act.wait_ge(x_summed.sem, x_summed.after(0, 0))
            act.activation(x_acc[:, :], probs_b[:, :], ACT.Ln, scale=1.0 / D_MODEL, bias=eps[:, :]).then_inc(act_setup, 1)
            act.wait_ge(act_setup, 2)
            act.activation(x_acc[:, :], x_acc[:, :], ACT.Exp, scale=-0.5).then_inc(x_rstd.sem, 1)
            for k in range(KT):
                round_h(0, k)
            for w in range(2):
                split_hi(0, w)

            with act.Fori(0, TILES) as t:
                for s in range(WT):
                    g, c = s - PAIR0, s - SCORES0
                    if 1 <= g <= G:
                        o = tok_b[:, 2 * P:3 * P]
                        act.wait_ge(o_done.sem, o_done.after(t, g - 1))
                        act.wait_ge(o_turned.sem, o_turned.after(t, g - 2))
                        then(t, act.activation(o_tok[:, :], o, ACT.Square, accum_out=o_sq[:, :]))
                        then(t, rstd(t, o_sq[:, :], o_sq[:, :], P))
                        act.activation(o_tok[:, :], o, ACT.Copy, scale=o_sq[:, :]).then_inc(o_normed.sem, 1)
                    if s - 1 in ROPE_TILES:
                        r = ROPE_TILES.index(s - 1)
                        src, dst = ((f_a, f_b), (f_c, f_d))[r % 2]
                        act.wait_ge(tile_read.sem, tile_read.after(t, s - 1))
                        for b in range(4):
                            act.dma_start(dst[32 * b:32 * b + 32, :],
                                          src[32 * (b ^ 1):32 * (b ^ 1) + 32, :]).then_inc(swapped[r % 2], 16)
                    if 0 <= s - 1 - Z0 < QT:
                        gate_first(t, s - 1, s - 1 - Z0)
                    if s + 2 < OUT0 + 4:
                        split_hi(t, s + 2)
                    if H0 < s <= OUT0:
                        h, kind = divmod(s - 1 - H0, 4)
                        if kind == 0:
                            act.wait_ge(tile_done.sem, tile_done.after(t, forget(h)))
                            act.wait_ge(k_dec_done.sem, k_dec_done.after(t, h - 1))
                            act.wait_ge(roped.sem, roped.after(t, QT))
                            log1p_exp(t, acc(forget(h))[:, :], f_a[:, :]).then_inc(f_ln.sem, 1)
                        if kind == 1:
                            act.wait_ge(f_scan.sem, f_scan.after(t, h))
                            act.activation(f_d[:, :], f_c[:, :], ACT.Exp)
                            act.activation(f_b[:, :], f_c[:, :], ACT.Exp, scale=-1.0).then_inc(f_exp.sem, 1)
                        if kind == 3:
                            gate_first(t, gate(h), QT + h)
                    if 1 <= c <= CHUNKS:
                        act.wait_ge(turned.sem, turned.after(t, c - 1))
                        act.activation(v_tok[:, :], att_b[:, 2 * P:3 * P], ACT.Copy)
                        act.activation(probs_t[:, :], probs_b[:, :], ACT.Copy).then_inc(p_turned.sem, 1)
                    if 0 <= s - 1 - Z0 < QT:
                        gate_second(t, s - 1 - Z0)
                    if H0 < s <= OUT0:
                        h, kind = divmod(s - 1 - H0, 4)
                        if kind == 0:
                            act.wait_ge(tile_read.sem, tile_read.after(t, forget(h)))
                            act.activation(f_a[:, :], f_a[:, :], ACT.Exp).then_inc(f_sig.sem, 1)
                    if 0 <= g < G:
                        act.wait_ge(to_tok.sem, to_tok.after(t, g))
                        act.activation(v_rtok[:, :], tok_b[:, P:2 * P], ACT.Copy)
                        act.activation(k_tok[0:64, 0, :], tok_b[0:64, 0:P], ACT.Copy)
                        act.activation(k_tok[64:128, 1, :], tok_b[64:128, 0:P], ACT.Copy).then_inc(kv_ready.sem, 1)
                    if 0 <= c < CHUNKS:
                        act.wait_ge(m_sub.sem, m_sub.after(t, c))
                        act.activation(sink_d[:, :], sink_d[:, :], ACT.Exp, scale=SCALE)
                        act.activation(probs[:, c % 2, :, :], probs[:, c % 2, :, :], ACT.Exp, scale=SCALE).then_inc(p_exp.sem, 1)
                    if H0 < s <= OUT0:
                        h, kind = divmod(s - 1 - H0, 4)
                        if kind == 0:
                            act.wait_ge(f_gate.sem, f_gate.after(t, h))
                            act.activation(f_b[:, :], f_b[:, :], ACT.Ln).then_inc(f_log.sem, 1)
                        if kind == 1:
                            act.wait_ge(f_rel.sem, f_rel.after(t, h))
                            act.activation(decay[:, h % 2, :], g_last[:, :], ACT.Exp)
                            act.activation(f_c[:, :], f_c[:, :], ACT.Exp).then_inc(f_end.sem, 1)
                        if kind == 3:
                            gate_second(t, QT + h)
                    j = s - (SCORES0 + CHUNKS + 1)
                    if 0 <= j < QT:
                        act.wait_ge(gated.sem, gated.after(t, CHUNKS - 1))
                        act.activation(mix_hi[:, j, :], q_gate[:, QT + j, :], ACT.Copy).then_inc(mixa_hi.sem, 1)
                    if 1 <= g <= G and g % PAIRS == 0:
                        h = g // PAIRS - 1
                        act.wait_ge(head_mixed.sem, head_mixed.after(t, h))
                        act.activation(mix_hi[:, QT + h, :], h_mix[:, :], ACT.Copy).then_inc(mixh_hi.sem, 1)
                    if 0 <= s - XSQ0 < KT:
                        square_x(t + 1, s - XSQ0)
                    if s == XSUM:
                        act.wait_ge(x_summed.sem, x_summed.after(t + 1, 0))
                        rstd(t, probs_b[:, :], x_acc[:, :], D_MODEL).then_inc(x_rstd.sem, 1)
                    if 0 <= s - H_NEW0 < KT // 2:
                        for k in (2 * (s - H_NEW0), 2 * (s - H_NEW0) + 1):
                            round_h(t + 1, k)
                    if s == OUT0 + 3:
                        for n in range(4):
                            square_y(t, n)
                            split_hi(t, OUT0 + 4 + n)
                    if s > OUT0 + 4:
                        square_y(t, s - 1 - OUT0)
                split_hi(t + 1, 0)
                square_y(t, KT - 1)
                split_hi(t + 1, 1)
                act.wait_ge(y_summed.sem, y_summed.after(t, 0))
                rstd(t, att_b[:, :], g_a[:, :], D_MODEL).then_inc(y_rstd.sem, 1)
            assert links[0] == act_step.per_tile, links[0]

        @block.vector
        def _(dve):
            for c in (tile_read, roped, gate_arg, f_gate, f_scan, f_rel, a_masked, state_b, state_c, mixed,
                      head_mixed, m_sub, p_inv, gated, h_scaled, h_lo_done, y_scaled, y_even, dve_step):
                c.start(dve)
            links = [0]

            def then(tile, instruction):
                instruction.then_inc(dve_step.sem, 1)
                dve.wait_ge(dve_step.sem, dve_step.after(tile, links[0]))
                links[0] += 1

            def scale_h(tile, k):
                if k == 0:
                    dve.wait_ge(x_rstd.sem, x_rstd.after(tile, 0))
                dve.scalar_tensor_tensor(x_in[:, k, :], x_in[:, k, :], w_pre[:, k:k + 1], x_acc[:, :],
                                         ALU.mult, ALU.mult).then_inc(h_scaled.sem, 1)

            def low_h(tile, k):
                dve.wait_ge(h_hi_done.sem, h_hi_done.after(tile, k))
                dve.tensor_tensor(h_lo[:, k, :], x_in[:, k, :], h_hi[:, k, :], ALU.subtract).then_inc(h_lo_done.sem, 1)

            dve.memset(ones[:, :], 1.0).then_inc(dve_setup, 1)
            dve.memset(eps[:, :], EPS)
            dve.memset(carry[:, :, :], 0.0)
            dve.memset(k_t[:, :, :], 0.0)
            dve.memset(k_tok[:, :, :], 0.0)
            dve.memset(v_t[:, 0:CHUNK], 0.0)
            dve.memset(a_t[:, :], 0.0)
            dve.memset(first_mask[:, 0:CHUNK], NEG_INF)
            dve.memset(first_mask[:, CHUNK:P], 0.0)
            dve.memset(reset[:, :].rearrange("p (c n) -> p c n", n=CHUNK)[:, :, 1:CHUNK], 1.0)
            dve.memset(reset[:, :].rearrange("p (c n) -> p c n", n=CHUNK)[:, :, 0:1], 0.0)
            dve.wait_ge(stored[0], 16)
            dve.wait_ge(stored[1], 16)
            dve.tensor_tensor(lb_m[:, :], lb_in[:, 0:HEADS], lb_in[:, HEADS:], ALU.max).then_inc(lb_step, 1)
            dve.wait_ge(lb_step, 1)
            dve.tensor_tensor(lb_e[:, 0:HEADS], lb_in[:, 0:HEADS], lb_m[:, :], ALU.subtract)
            dve.tensor_tensor(lb_e[:, HEADS:], lb_in[:, HEADS:], lb_m[:, :], ALU.subtract).then_inc(dve_setup, 1)
            dve.wait_ge(act_setup, 1)
            dve.tensor_tensor(lb_m[:, :], lb_e[:, 0:HEADS], lb_e[:, HEADS:], ALU.add).then_inc(lb_step, 1)
            dve.wait_ge(lb_step, 2)
            dve.reciprocal(lb_m[:, :], lb_m[:, :]).then_inc(lb_step, 1)
            dve.wait_ge(lb_step, 3)
            dve.tensor_tensor(lb[:, :], lb_e[:, 0:HEADS], lb_m[:, :], ALU.mult).then_inc(lb_step, 1)
            dve.wait_ge(lb_step, 4)
            dve.tensor_scalar(lb_rest[:, :], lb[:, :], -1.0, 1.0, ALU.mult, ALU.add)
            dve.tensor_scalar(sink8[:, :], sink_in, 1.0 / SCALE, None, ALU.mult)
            for k in range(KT):
                scale_h(0, k)
            for k in range(KT):
                low_h(0, k)

            def per_chunk(ap):
                return ap.rearrange("p (c n) -> p c n", n=CHUNK)

            def rope_copy(t, r):
                w = ROPE_TILES[r]
                src = (f_a, f_c)[r % 2]
                dve.wait_ge(tile_done.sem, tile_done.after(t, w))
                dve.wait_ge(k_dec_done.sem, k_dec_done.after(t, -1))
                dve.wait_ge(roped.sem, roped.after(t, r - 2))
                dve.tensor_copy(src[:, :], acc(w)[:, :]).then_inc(tile_read.sem, 1)

            def rope_turn(t, r):
                a, b = ((f_a, f_b), (f_c, f_d))[r % 2]
                if r == 0:
                    dve.wait_ge(tables_loaded, t * 32 + 32)
                dve.wait_ge(*loaded(swapped[r % 2], (3, 2)[r % 2], t, r // 2, 4))
                dve.tensor_tensor(a[:, :], a[:, :], cos_t[:, :], ALU.mult)
                then(t, dve.tensor_tensor(b[:, :], b[:, :], sin_t[:, :], ALU.mult))
                if r == 0:
                    for g in range(2):
                        rows = slice(64 * g, 64 * g + 64)
                        last = dve.tensor_tensor(k_t[rows, g, CHUNK:], a[rows, :], b[rows, :], ALU.add)
                else:
                    dve.wait_ge(stored[0], t * 16 + 16)
                    last = dve.tensor_tensor(queries[:, (r - 1) // 2, :, (r - 1) % 2, :], per_chunk(a[:, :]),
                                             per_chunk(b[:, :]), ALU.add)
                last.then_inc(roped.sem, 1)

            def gate_first(t, w, i):
                dve.wait_ge(gate_ln.sem, gate_ln.after(t, i))
                dve.scalar_tensor_tensor(g_a[:, :], acc(w)[:, :], 0.0, g_a[:, :], ALU.min, ALU.subtract).then_inc(gate_arg.sem, 1)

            def gate_second(t, w, i, dst):
                dve.wait_ge(gate_sig.sem, gate_sig.after(t, i))
                dve.tensor_tensor(dst, acc(w)[:, :], g_a[:, :], ALU.mult).then_inc(tile_read.sem, 1)

            def copy_y(t, n):
                dve.wait_ge(y_squared.sem, y_squared.after(t, n))
                dve.tensor_copy(q_gate[:, n, :], acc(OUT0 + n)[:, :]).then_inc(tile_read.sem, 1)

            with dve.Fori(0, TILES) as t:
                for s in range(WT):
                    g, c = s - PAIR0, s - SCORES0
                    h_of, kind = divmod(s - 1 - H0, 4) if H0 < s <= OUT0 else (0, None)
                    if s - 1 in ROPE_TILES:
                        rope_copy(t, ROPE_TILES.index(s - 1))
                    if s - 1 == V_TILE:
                        dve.wait_ge(tile_done.sem, tile_done.after(t, V_TILE))
                        dve.tensor_copy(v_t[:, CHUNK:], acc(V_TILE)[:, :]).then_inc(tile_read.sem, 1)
                    if kind == 2:
                        dve.wait_ge(tile_done.sem, tile_done.after(t, query(h_of)))
                        dve.wait_ge(o_done.sem, o_done.after(t, PAIRS * h_of - 1))
                        dve.tensor_tensor(q_dec[:, :], acc(query(h_of))[:, :], f_d[:, :], ALU.mult).then_inc(tile_read.sem, 1)
                        dve.wait_ge(tile_done.sem, tile_done.after(t, value(h_of)))
                        dve.tensor_copy(v_r[:, :], acc(value(h_of))[:, :]).then_inc(tile_read.sem, 1)
                    if s - 2 in ROPE_TILES:
                        rope_turn(t, ROPE_TILES.index(s - 2))
                    if 0 <= s - 1 - Z0 < QT:
                        gate_first(t, s - 1, s - 1 - Z0)
                    if kind == 0:
                        dve.wait_ge(f_ln.sem, f_ln.after(t, h_of))
                        dve.scalar_tensor_tensor(f_a[:, :], acc(forget(h_of))[:, :], 0.0, f_a[:, :], ALU.min,
                                                 ALU.subtract).then_inc(tile_read.sem, 1)
                    if kind == 1:
                        dve.wait_ge(f_exp.sem, f_exp.after(t, h_of))
                        then(t, dve.tensor_copy(g_last[:, :], per_chunk(f_c[:, :])[:, :, CHUNK - 1]))
                        dve.tensor_tensor(per_chunk(f_c[:, :]), g_last[:, :].unsqueeze(2).broadcast_to([P, CHUNKS, CHUNK]),
                                          per_chunk(f_c[:, :]), ALU.subtract).then_inc(f_rel.sem, 1)
                    if kind == 3:
                        gate_first(t, gate(h_of), QT + h_of)
                    if 0 <= c < CHUNKS:
                        pr = probs[:, c % 2, :, :]
                        src = score_b[:, :].rearrange("p (b m) -> p b m", b=4)
                        dve.wait_ge(scored.sem, scored.after(t, c))
                        if c == 0:
                            then(t, dve.tensor_tensor(pr, src, first_mask[:, :].unsqueeze(1).broadcast_to([P, 4, P]), ALU.add))
                            src = pr
                        then(t, dve.reduce_max(top[:, :], src, axis=AX.X))
                        then(t, dve.tensor_tensor(s_max[:, :], top[:, :], sink8[:, :], ALU.max))
                        dve.tensor_tensor(sink_d[:, :], sink8[:, :], s_max[:, :], ALU.subtract)
                        dve.tensor_tensor(pr, src, s_max[:, :].unsqueeze(2).broadcast_to([P, 4, P]), ALU.subtract).then_inc(m_sub.sem, 1)
                        if c == 0:
                            dve.memset(first_mask[:, 0:CHUNK], 0.0)
                    if 1 <= g <= G:
                        h, p = divmod(g - 1, PAIRS)
                        dve.wait_ge(o_turned.sem, o_turned.after(t, g - 1))
                        if p == 0:
                            dve.wait_ge(mixh_lo.sem, mixh_lo.after(t, h - 1))
                        dve.tensor_scalar(h_mix[:, pair(p)], pair_b[:, 3 * P:4 * P], w_head, None, ALU.mult).then_inc(mixed.sem, 1)
                        if p == PAIRS - 1:
                            dve.wait_ge(mixed.sem, mixed.after(t, g - 1))
                            dve.tensor_tensor(h_mix[:, :], h_mix[:, :], z_r[:, :], ALU.mult).then_inc(head_mixed.sem, 1)
                    if 0 <= s - 1 - Z0 < QT:
                        dve.wait_ge(stored[1], t * 16 + 16)
                        gate_second(t, s - 1, s - 1 - Z0, q_gate[:, s - 1 - Z0 + QT, :])
                    if kind == 0:
                        dve.wait_ge(f_sig.sem, f_sig.after(t, h_of))
                        then(t, dve.tensor_scalar(f_b[:, :], f_a[:, :], lb_rest[:, h_of:h_of + 1], lb[:, h_of:h_of + 1],
                                                  ALU.mult, ALU.add))
                        dve.tensor_scalar(f_a[:, :], f_b[:, :], -1.0, 1.0, ALU.mult, ALU.add).then_inc(f_gate.sem, 1)
                    if 0 <= c < CHUNKS:
                        dve.wait_ge(p_exp.sem, p_exp.after(t, c))
                        dve.wait_ge(p_normed.sem, p_normed.after(t, c - 1))
                        then(t, dve.reduce_sum(s_sum[:, :], probs[:, c % 2, :, :], axis=AX.X))
                        then(t, dve.tensor_tensor(s_sum[:, :], s_sum[:, :], sink_d[:, :], ALU.add))
                        dve.reciprocal(s_inv[:, :], s_sum[:, :]).then_inc(p_inv.sem, 1)
                    if 1 <= c <= CHUNKS:
                        gates = q_gate[:, QT:, chunk(c - 1)]
                        dve.wait_ge(weighed.sem, weighed.after(t, c - 1))
                        if c == 1:
                            dve.wait_ge(tile_read.sem, tile_read.after(t, Z0 + QT - 1))
                        dve.tensor_tensor(gates, att_b[:, 0:2 * P].rearrange("p (j n) -> p j n", j=QT), gates,
                                          ALU.mult).then_inc(gated.sem, 1)
                        if c == CHUNKS:
                            dve.tensor_copy(k_t[:, :, 0:CHUNK], k_t[:, :, N:])
                            dve.tensor_copy(v_t[:, 0:CHUNK], v_t[:, N:])
                    if 0 <= g < G:
                        h, p = divmod(g, PAIRS)
                        a = carry[:, h, :] if p == 0 else ring[:, (2 * p + 3) % 4, :]
                        m = ring[:, (2 * p) % 4, :]
                        z = carry[:, h, :] if p == PAIRS - 1 else ring[:, (2 * p + 1) % 4, :]
                        dve.wait_ge(a_u.sem, a_u.after(t, g))
                        dve.scalar_tensor_tensor(m, a, decay[:, h % 2, 2 * p:2 * p + 1], pair_b[:, P:2 * P],
                                                 ALU.mult, ALU.add).then_inc(state_b.sem, 1)
                        dve.copy_predicated(a_t[:, :], causal, pair_b[:, 0:P]).then_inc(a_masked.sem, 1)
                        dve.wait_ge(state_b.sem, state_b.after(t, g))
                        dve.scalar_tensor_tensor(z, m, decay[:, h % 2, 2 * p + 1:2 * p + 2], pair_b[:, 2 * P:3 * P],
                                                 ALU.mult, ALU.add).then_inc(state_c.sem, 1)
                    if kind == 0:
                        dve.wait_ge(f_log.sem, f_log.after(t, h_of))
                        dve.tensor_tensor_scan(f_c[:, :], reset[:, :], f_b[:, :], 0.0, ALU.mult, ALU.add).then_inc(f_scan.sem, 1)
                    if kind == 3:
                        gate_second(t, gate(h_of), QT + h_of, z_r[:, :])
                    if 0 <= s - H_NEW0 < KT // 2:
                        for k in (2 * (s - H_NEW0), 2 * (s - H_NEW0) + 1):
                            scale_h(t + 1, k)
                        for k in (2 * (s - H_NEW0), 2 * (s - H_NEW0) + 1):
                            low_h(t + 1, k)
                    if s == OUT0 + 3:
                        for n in range(4):
                            copy_y(t, n)
                    if s > OUT0 + 4:
                        copy_y(t, s - 1 - OUT0)
                copy_y(t, KT - 1)
                dve.wait_ge(tile_read.sem, tile_read.after(t, WT - 1))
                dve.wait_ge(y_rstd.sem, y_rstd.after(t, 0))
                for n in range(KT):
                    y = q_gate[:, n, :]
                    dve.scalar_tensor_tensor(y, y, w_post[:, n:n + 1], g_a[:, :], ALU.mult, ALU.mult).then_inc(y_scaled.sem, 1)
                for n in range(0, KT, 2):
                    y = q_gate[:, n, :]
                    dve.wait_ge(y_scaled.sem, y_scaled.after(t, n))
                    dve.wait_ge(res_loaded, t * 16 + 16)
                    dve.tensor_tensor(y, y, x_in[:, n, :], ALU.add).then_inc(y_even.sem, 1)
            assert links[0] == dve_step.per_tile, links[0]

        @block.gpsimd
        def _(pool):
            for c in (lo_split, k_dec_done, k_end_done, p_normed, mixa_lo, mixh_lo, x_added, y_added, y_odd):
                c.start(pool)
            pool.dma_start(vec[:, :], vectors).then_inc(stored[0], 16)
            pool.dma_start(sq_in[:, :, :], squares.rearrange("p (a b) -> p a b", a=2)).then_inc(stored[1], 16)

            def split_lo(tile, w):
                pool.wait_ge(hi_split.sem, hi_split.after(tile, w))
                s = w % SLOTS
                pool.tensor_tensor(w_lo[:, s, :, :], w_raw[:, s, :, :], w_hi[:, s, :, :], ALU.subtract).then_inc(lo_split.sem, 1)

            def add_x(tile, k):
                pool.wait_ge(x_squared.sem, x_squared.after(tile, k))
                pool.wait_ge(x_added.sem, x_added.after(tile, k - 2))
                pool.tensor_tensor(x_acc[:, :], x_acc[:, :], x_sq[:, :], ALU.add).then_inc(x_added.sem, 1)

            def add_y(t, n):
                pool.wait_ge(y_squared.sem, y_squared.after(t, n))
                pool.wait_ge(y_added.sem, y_added.after(t, n - 2))
                pool.tensor_tensor(f_c[:, :], f_c[:, :], (g_a, f_d)[n % 2][:, :], ALU.add).then_inc(y_added.sem, 1)

            for k in range(1, KT):
                add_x(0, k)
            for w in range(2):
                split_lo(0, w)
            with pool.Fori(0, TILES) as t:
                for s in range(WT):
                    g, c = s - PAIR0, s - SCORES0
                    h_of, kind = divmod(s - 1 - H0, 4) if H0 < s <= OUT0 else (0, None)
                    if kind == 2:
                        pool.wait_ge(f_exp.sem, f_exp.after(t, h_of))
                        pool.wait_ge(a_u.sem, a_u.after(t, PAIRS * h_of - 1))
                        pool.tensor_tensor(k_dec[:, :], f_a[:, :], f_b[:, :], ALU.mult).then_inc(k_dec_done.sem, 1)
                    if s + 2 < OUT0 + 4:
                        split_lo(t, s + 2)
                    if 0 <= c < CHUNKS:
                        pr = probs[:, c % 2, :, :]
                        pool.wait_ge(p_inv.sem, p_inv.after(t, c))
                        pool.tensor_tensor(pr, pr, s_inv[:, :].unsqueeze(2).broadcast_to([P, 4, P]), ALU.mult).then_inc(p_normed.sem, 1)
                    if kind == 1:
                        pool.wait_ge(f_end.sem, f_end.after(t, h_of))
                        pool.wait_ge(to_tok.sem, to_tok.after(t, PAIRS * h_of - 1))
                        pool.tensor_tensor(k_end[:, :], f_a[:, :], f_c[:, :], ALU.mult).then_inc(k_end_done.sem, 1)
                    j = s - (SCORES0 + CHUNKS + 1)
                    if 0 <= j < QT:
                        pool.wait_ge(mixa_hi.sem, mixa_hi.after(t, j))
                        pool.tensor_tensor(mix_lo[:, j, :], q_gate[:, QT + j, :], mix_hi[:, j, :], ALU.subtract).then_inc(mixa_lo.sem, 1)
                    if 1 <= g <= G and g % PAIRS == 0:
                        h = g // PAIRS - 1
                        pool.wait_ge(mixh_hi.sem, mixh_hi.after(t, h))
                        pool.tensor_tensor(mix_lo[:, QT + h, :], h_mix[:, :], mix_hi[:, QT + h, :],
                                           ALU.subtract).then_inc(mixh_lo.sem, 1)
                    if 0 < s - XSQ0 < KT:
                        add_x(t + 1, s - XSQ0)
                    if s == OUT0 + 3:
                        for n in range(4):
                            split_lo(t, OUT0 + 4 + n)
                            if n:
                                add_y(t, n)
                    if s > OUT0 + 4:
                        add_y(t, s - 1 - OUT0)
                for w in range(2):
                    split_lo(t + 1, w)
                for n in range(1, KT, 2):
                    y = q_gate[:, n, :]
                    pool.wait_ge(y_scaled.sem, y_scaled.after(t, n))
                    pool.wait_ge(res_loaded, t * 16 + 16)
                    pool.tensor_tensor(y, y, x_in[:, n, :], ALU.add).then_inc(y_odd.sem, 1)
                    if n % 4 == 3:
                        half = n // 4
                        pool.wait_ge(y_odd.sem, y_odd.after(t, n // 2))
                        pool.wait_ge(y_even.sem, y_even.after(t, n // 2))
                        pool.dma_start(out[bass.ts(t, P), 4 * half * N:4 * (half + 1) * N].rearrange("p (k n) -> p k n", n=N),
                                       q_gate[:, 4 * half:4 * half + 4, :]).then_inc(stored[half], 16)


def weight_tiles(w_in, w_out):
    head = lambda start, j: slice(start + 64 * j, start + 64 * j + 64)
    starts = np.cumsum([0, 512, 128, 128, 512, 512, 512, 512])
    q_a, k_a, v_a, z_a, q_r, f_r, i_r, z_r = (int(v) for v in starts)
    columns = [w_in[:, k_a:k_a + P], w_in[:, v_a:v_a + P]]
    for start in (q_a, z_a):
        columns += [w_in[:, head(start, j + QT * g)] for j in range(QT) for g in range(2)]
    for h in range(HEADS):
        columns += [w_in[:, start + P * h:start + P * (h + 1)] for start in (f_r, q_r, i_r, z_r)]
    columns = np.concatenate(columns, axis=1).reshape(KT, P, OUT0, P).transpose(2, 1, 0, 3)
    rows = [w_out[head(0, j + QT * g)] for j in range(QT) for g in range(2)] + [w_out[512:]]
    rows = np.concatenate(rows, axis=0).reshape(KT, P, KT, P).transpose(2, 1, 0, 3)
    return np.concatenate([columns, rows], axis=0).reshape(WT * P, KT * P)


def rope_tables():
    half = 32
    inv = np.float32(ROPE_THETA) ** (-np.arange(half, dtype=np.float32) / np.float32(half))
    angle = inv[:, None] * np.arange(SEQ, dtype=np.float32)[None, :]
    cos, sin = np.cos(angle), np.sin(angle)
    cos, sin = np.concatenate([cos] * 4, axis=0), np.concatenate([-sin, sin, -sin, sin], axis=0)
    tiled = lambda a: np.ascontiguousarray(a.reshape(P, TILES, N).transpose(1, 0, 2).reshape(TILES * P, N), dtype=np.float32)
    return tiled(cos), tiled(sin)


def kernel(x, w_norm_pre, w_in, attn_sinks, hgrn_lb, hgrn_norm, w_out, w_norm_post):
    import concourse.bacc as bacc
    from concourse.bass_utils import run_bass_kernel_spmd

    x = np.asarray(x)
    by_tile = x[0].reshape(TILES, N, KT, P).transpose(0, 3, 2, 1).reshape(TILES * P, KT * N)
    cos, sin = rope_tables()
    by_partition = lambda v: np.asarray(v).reshape(-1, P).T
    sinks = np.repeat(np.asarray(attn_sinks)[0].reshape(2, 2, 2).transpose(2, 0, 1).reshape(2, 4), CHUNK, axis=0)
    vectors = np.concatenate([by_partition(w_norm_pre), by_partition(w_norm_post), by_partition(hgrn_norm),
                              by_partition(hgrn_lb), sinks], axis=1)
    m, l = np.arange(P)[:, None], np.arange(P)[None, :]
    squares = np.concatenate([np.eye(P), (m // CHUNK == l // CHUNK) & (l >= m)], axis=1).astype(np.float32)
    arrays = {
        "x": by_tile, "weights": weight_tiles(np.asarray(w_in)[0], np.asarray(w_out)[0]),
        "cos": cos, "sin": sin, "vectors": vectors, "squares": squares,
    }
    arrays = {f"in_{name}": np.ascontiguousarray(a) for name, a in arrays.items()}

    nc = bacc.Bacc("TRN2", target_bir_lowering=False, num_devices=1)
    aps = [nc.dram_tensor(name, a.shape, FP32, kind="ExternalInput").ap() for name, a in arrays.items()]
    out = nc.dram_tensor("out", by_tile.shape, FP32, kind="ExternalOutput").ap()
    hybrid_block(nc, *aps, out)
    got = run_bass_kernel_spmd(nc, [arrays], core_ids=[0]).results[0]["out"]
    return got.reshape(TILES, P, KT, N).transpose(0, 3, 2, 1).reshape(1, SEQ, D_MODEL)
```

```python
import math
from contextlib import ExitStack

import numpy as np
import concourse.bass as bass
from concourse import mybir

FP32 = mybir.dt.float32
FP32R = mybir.dt.float32r
INT32 = mybir.dt.int32
ALU = mybir.AluOpType
ACT = mybir.ActivationFunctionType
AX = mybir.AxisListType

P = 128
SEQ, D_MODEL = 2048, 1024
N = 512
TILES = SEQ // N
KT = D_MODEL // P
CHUNK = 64
CHUNKS = N // CHUNK
PAIRS = N // P
HEADS = 4
QT = 4
EPS = 1e-6
NEG_INF = -1e30
SCALE = 0.125
ROPE_THETA = 10000.0

K_TILE, V_TILE = 0, 1
Q0, Z0 = 2, 2 + QT
H0 = Z0 + QT
OUT0 = H0 + 4 * HEADS
WT = OUT0 + KT
ROPE_TILES = [K_TILE] + [Q0 + j for j in range(QT)]
RAW_SLOTS, AHEAD = 4, 3
RAW_SLOT = [w % RAW_SLOTS for w in range(WT)]
SPLIT_SLOT = [s for r in (4, 4, 4, 4, 4, 5, 5, 4) for s in range(r)]
RAW_USES = [RAW_SLOT.count(s) for s in range(RAW_SLOTS)]
assert len(SPLIT_SLOT) == WT and OUT0 == 26

SCORES0 = Z0 + 3
PAIR0 = H0 + 3
XSQ0 = PAIR0 + 5
XSUM = XSQ0 + KT
H_PARTS = {XSUM + 1: (0, 1, 2), XSUM + 2: (3, 4, 5), XSUM + 3: (6, 7)}
Y_POOL = (2, 5)
Y_DVE = tuple(n for n in range(KT) if n not in Y_POOL)


def forget(h):
    return H0 + 4 * h


def query(h):
    return H0 + 4 * h + 1


def value(h):
    return H0 + 4 * h + 2


def gate(h):
    return H0 + 4 * h + 3


def before(w, slot):
    return next(v for v in range(w - 1, w - WT - 1, -1) if slot[v % WT] == slot[w])


class Count:

    def __init__(self, sem, per_tile):
        self.sem, self.per_tile = sem, per_tile

    def start(self, engine):
        engine.sem_inc(self.sem, self.per_tile)

    def after(self, tile, i):
        assert -self.per_tile <= i < self.per_tile
        return tile * self.per_tile + (self.per_tile + i + 1)


def hybrid_block(nc, x, weights, cos, sin, vectors, squares, out):
    ctx = ExitStack()
    with ctx:
        def sb(name, shape, dt=FP32):
            return ctx.enter_context(nc.sbuf_tensor(name, [P] + shape, dt))

        def sem(name):
            return ctx.enter_context(nc.semaphore(name))

        x_in = sb("x_in", [KT, N])
        h_hi, h_lo = sb("h_hi", [KT, N], FP32R), sb("h_lo", [KT, N], FP32R)
        mix_hi, mix_lo = sb("mix_hi", [KT, N], FP32R), sb("mix_lo", [KT, N], FP32R)
        w_raw = sb("w_raw", [RAW_SLOTS, KT, P])
        w_hi, w_lo = (sb(n, [max(SPLIT_SLOT) + 1, KT, P], FP32R) for n in ("w_hi", "w_lo"))
        q_gate = sb("q_gate", [2 * QT, N])
        queries = q_gate[:, 0:QT, :].rearrange("p q n -> p (q n)").rearrange(
            "p (h c j n) -> p h c j n", h=2, c=CHUNKS, j=2)
        k_t = sb("k_t", [2, CHUNK + N])
        v_t = sb("v_t", [CHUNK + N])
        cos_t, sin_t = sb("cos_t", [N]), sb("sin_t", [N])
        f_a, f_b, f_c, f_d = (sb(f"f_{c}", [N]) for c in "abcd")
        g_a = sb("g_a", [N])
        q_dec, k_dec, k_end = sb("q_dec", [N]), sb("k_dec", [N]), sb("k_end", [N])
        v_r, z_r, h_mix = sb("v_r", [N]), sb("z_r", [N]), sb("h_mix", [N])
        probs = sb("probs", [2, 4, P])
        probs_t = sb("probs_t", [N])
        v_tok = sb("v_tok", [P])
        k_tok = sb("k_tok", [2, P])
        v_rtok = sb("v_rtok", [P])
        a_t = sb("a_t", [P])
        o_tok = sb("o_tok", [P])
        carry = sb("carry", [HEADS, P])
        ring = sb("ring", [4, P])
        x_sq, x_acc = sb("x_sq", [N]), sb("x_acc", [N])
        reset = sb("reset", [N])
        ones = sb("ones", [P])
        sq_in = sb("sq_in", [2, P])
        ident = sq_in[:, 0, :]
        causal = sq_in[:, 1, :].bitcast(INT32)
        first_mask = sb("first_mask", [P])
        vec = sb("vec", [2 * KT + 1 + 2 * HEADS + 4])
        w_pre, w_post = vec[:, 0:KT], vec[:, KT:2 * KT]
        w_head = vec[:, 2 * KT:2 * KT + 1]
        lb_in = vec[:, 2 * KT + 1:2 * KT + 1 + 2 * HEADS]
        sink_in = vec[:, 2 * KT + 1 + 2 * HEADS:]
        lb, lb_rest = sb("lb", [HEADS]), sb("lb_rest", [HEADS])
        lb_e = sb("lb_e", [2 * HEADS])
        lb_m = sb("lb_m", [HEADS])
        sink8 = sb("sink8", [4])
        g_last = sb("g_last", [CHUNKS])
        decay = sb("decay", [2, CHUNKS])
        top, s_max, s_sum, s_inv = (sb(n, [4]) for n in ("top", "s_max", "s_sum", "s_inv"))
        sink_d = sb("sink_d", [4])
        o_sq = sb("o_sq", [1])
        eps = sb("eps", [1])

        bank = [ctx.enter_context(nc.psum_tensor(f"bank{i}", [P, N], FP32)) for i in range(8)]
        score_b, probs_b, att_b, tok_b, pair_b = bank[3:]

        def acc(w):
            if w in (OUT0 + 3, WT - 1):
                return score_b
            order = [i for i in range(WT) if i not in (OUT0 + 3, WT - 1)]
            return bank[order.index(w) % 3]

        def acc_before(w):
            for v in range(w - 1, w - WT - 1, -1):
                if acc(v % WT) is acc(w):
                    return v

        x_first = [sem(f"x_first{k}") for k in range(KT)]
        x_loaded, tables_loaded = sem("x_loaded"), sem("tables_loaded")
        w_loaded = [sem(f"w_loaded{i}") for i in range(RAW_SLOTS)]
        swapped = [sem(f"swapped{i}") for i in range(2)]
        res_loaded = sem("res_loaded")
        stored = [sem(f"stored{i}") for i in range(2)]

        def count(name, per_tile):
            return Count(sem(name), per_tile)

        tile_done = count("tile_done", WT)
        x_summed, y_summed = count("x_summed", 1), count("y_summed", 1)
        scored, turned, weighed = (count(n, CHUNKS) for n in ("scored", "turned", "weighed"))
        G = HEADS * PAIRS
        to_tok, a_u, o_done, o_turned = (count(n, G) for n in ("to_tok", "a_u", "o_done", "o_turned"))
        hi_split = count("hi_split", WT)
        gate_ln, gate_sig = (count(n, QT + HEADS) for n in ("gate_ln", "gate_sig"))
        f_ln, f_sig, f_log, f_exp, f_end = (count(n, HEADS) for n in ("f_ln", "f_sig", "f_log", "f_exp", "f_end"))
        p_exp, p_turned = count("p_exp", CHUNKS), count("p_turned", CHUNKS)
        kv_ready, o_normed = count("kv_ready", G), count("o_normed", G)
        mixa_hi, mixh_hi = count("mixa_hi", QT), count("mixh_hi", HEADS)
        x_squared, h_hi_done = count("x_squared", KT), count("h_hi_done", KT)
        y_squared, x_rstd, y_rstd = count("y_squared", KT), count("x_rstd", 1), count("y_rstd", 1)
        act_step = count("act_step", 2 * (QT + HEADS) + 2 * HEADS + 3 * HEADS * PAIRS + 2)
        tile_read = count("tile_read", WT)
        roped = count("roped", len(ROPE_TILES))
        gate_arg = count("gate_arg", QT + HEADS)
        f_gate, f_scan, f_rel = (count(n, HEADS) for n in ("f_gate", "f_scan", "f_rel"))
        a_masked, state_b, state_c, mixed = (count(n, G) for n in ("a_masked", "state_b", "state_c", "mixed"))
        head_mixed = count("head_mixed", HEADS)
        m_sub, p_inv, gated = (count(n, CHUNKS) for n in ("m_sub", "p_inv", "gated"))
        h_scaled, h_lo_done = count("h_scaled", KT), count("h_lo_done", KT)
        y_done = count("y_done", len(Y_DVE))
        dve_step = count("dve_step", len(ROPE_TILES) + CHUNKS * 4 + 1 + HEADS * 2 + len(Y_DVE) // 2)
        dve_setup, lb_step = sem("dve_setup"), sem("lb_step")
        act_setup = sem("act_setup")
        lo_split = count("lo_split", WT)
        k_dec_done, k_end_done = count("k_dec_done", HEADS), count("k_end_done", HEADS)
        p_normed = count("p_normed", CHUNKS)
        mixa_lo, mixh_lo = count("mixa_lo", QT), count("mixh_lo", HEADS)
        x_added, y_added = count("x_added", KT - 1), count("y_added", KT - 2)
        y_scaled, y_pool_done = count("y_scaled", len(Y_POOL)), count("y_pool_done", len(Y_POOL))
        first_low, sq_added = sem("first_low"), sem("sq_added")

        def loaded(sems, uses, tile, i, n=1):
            return (sems, tile * (16 * n * uses) + 16 * n * (i + 1))

        def wait_weights(engine, tile, w):
            engine.wait_ge(*loaded(w_loaded[RAW_SLOT[w]], RAW_USES[RAW_SLOT[w]], tile, w // RAW_SLOTS))

        def chunk(c, n=1):
            return slice(c * CHUNK, (c + n) * CHUNK)

        def pair(p):
            return slice(p * P, (p + 1) * P)

        block = ctx.enter_context(nc.Block())

        @block.sync
        def _(sp):
            def load_x(tile, row):
                sp.wait_ge(h_lo_done.sem, h_lo_done.after(tile, -1))
                sp.wait_ge(y_done.sem, y_done.after(tile - 1, -1))
                sp.wait_ge(y_pool_done.sem, y_pool_done.after(tile - 1, -1))
                sp.dma_start(x_in[:, :, :], x[bass.ts(row, P), :].rearrange("p (k n) -> p k n", k=KT)).then_inc(x_loaded, 16)

            def load_weights(tile, w):
                sp.wait_ge(lo_split.sem, lo_split.after(tile, before(w, RAW_SLOT)))
                sp.dma_start(w_raw[:, RAW_SLOT[w], :, :],
                             weights[w * P:(w + 1) * P, :].rearrange("p (k m) -> p k m", k=KT)).then_inc(w_loaded[RAW_SLOT[w]], 16)

            def load_residual(t, half):
                k = half * KT // 2
                sp.wait_ge(h_lo_done.sem, h_lo_done.after(t + 1, k + KT // 2 - 1))
                sp.dma_start(x_in[:, k:k + KT // 2, :], x[bass.ts(t, P), k * N:(k + KT // 2) * N].rearrange(
                    "p (k n) -> p k n", n=N)).then_inc(res_loaded, 16)

            for k in range(KT):
                sp.dma_start(x_in[:, k, :], x[0:P, k * N:(k + 1) * N]).then_inc(x_first[k], 16)
            with sp.Fori(0, TILES) as t:
                for w in range(WT):
                    load_weights(t, w)
                    if w == 0:
                        sp.wait_ge(roped.sem, roped.after(t, -1))
                        sp.dma_start(cos_t[:, :], cos[bass.ts(t, P), :]).then_inc(tables_loaded, 16)
                        sp.dma_start(sin_t[:, :], sin[bass.ts(t, P), :]).then_inc(tables_loaded, 16)
                    if w == H0:
                        load_x(t + 1, (t + 1) % TILES)
                    if w == WT - 3:
                        load_residual(t, 0)
                    if w == WT - 1:
                        load_residual(t, 1)
            for w in range(AHEAD):
                load_weights(TILES, w)
            for w in range(AHEAD):
                wait_weights(sp, TILES, w)
            for s in stored:
                sp.wait_ge(s, 32 * (TILES + 1))

        @block.tensor
        def _(pe):
            for c in (tile_done, x_summed, y_summed, scored, turned, weighed, to_tok, a_u, o_done, o_turned):
                c.start(pe)

            def sum_x(tile):
                pe.wait_ge(x_added.sem, x_added.after(tile, KT - 2))
                pe.matmul(probs_b[:, :], ones[:, :], x_acc[:, :], start=True, stop=True).then_inc(x_summed.sem, 1)

            def products(w, m, last):
                k, part = m // 3, m % 3
                s = SPLIT_SLOT[w]
                hi, lo = (h_hi, h_lo) if w < OUT0 else (mix_hi, mix_lo)
                stationary, moving = ((w_hi, hi), (w_lo, hi), (w_hi, lo))[part]
                mm = pe.matmul(acc(w)[:, :], stationary[:, s, k, :], moving[:, k, :],
                               start=(m == 0), stop=(m == 3 * KT - 1), skip_group_check=True)
                if last:
                    mm.then_inc(tile_done.sem, 1)

            def scores(t, c):
                if c == 0:
                    pe.wait_ge(roped.sem, roped.after(t, QT))
                    pe.wait_ge(tile_read.sem, tile_read.after(t, -1))
                else:
                    pe.wait_ge(m_sub.sem, m_sub.after(t, c - 1))
                for b in range(4):
                    g, hp = b // 2, b % 2
                    mm = pe.matmul(score_b[:, pair(b)], queries[:, hp, c, :, :].rearrange("p j n -> p (j n)"),
                                   k_t[:, g, chunk(c, 2)], start=True, stop=True)
                mm.then_inc(scored.sem, 1)

            def turn(t, c):
                pe.wait_ge(gated.sem, gated.after(t, c - 1))
                pe.transpose(att_b[:, 2 * P:3 * P], v_t[:, chunk(c, 2)], ident)
                pe.wait_ge(p_normed.sem, p_normed.after(t, c))
                for b in range(4):
                    mm = pe.transpose(probs_b[:, pair(b)], probs[:, c % 2, b, :], ident)
                mm.then_inc(turned.sem, 1)

            def weigh(t, c):
                pe.wait_ge(p_turned.sem, p_turned.after(t, c))
                for g in range(2):
                    mm = pe.matmul(att_b[64 * g:64 * g + 64, 0:2 * P], v_tok[:, 64 * g:64 * g + 64],
                                   probs_t[:, 2 * P * g:2 * P * (g + 1)], start=True, stop=True)
                mm.then_inc(weighed.sem, 1)

            def pair_to_tok(t, g):
                h, p = divmod(g, PAIRS)
                if p == 0:
                    pe.wait_ge(k_end_done.sem, k_end_done.after(t, h))
                    pe.wait_ge(tile_read.sem, tile_read.after(t, value(h)))
                pe.transpose(tok_b[:, 0:P], k_end[:, pair(p)], ident)
                pe.transpose(tok_b[:, P:2 * P], v_r[:, pair(p)], ident).then_inc(to_tok.sem, 1)

            def pair_products(t, g):
                h, p = divmod(g, PAIRS)
                if p == 0:
                    pe.wait_ge(k_dec_done.sem, k_dec_done.after(t, h))
                pe.wait_ge(mixed.sem, mixed.after(t, g - 1))
                pe.wait_ge(kv_ready.sem, kv_ready.after(t, g))
                pe.matmul(pair_b[:, 0:P], k_dec[:, pair(p)], q_dec[:, pair(p)], start=True, stop=True)
                pe.matmul(pair_b[:, P:2 * P], k_tok[:, 0, :], v_rtok[:, :], start=True, stop=True)
                pe.matmul(pair_b[:, 2 * P:3 * P], k_tok[:, 1, :], v_rtok[:, :], start=True, stop=True).then_inc(a_u.sem, 1)

            def states(g):
                h, p = divmod(g, PAIRS)
                a = carry[:, h, :] if p == 0 else ring[:, (2 * p + 3) % 4, :]
                c = carry[:, h, :] if p == PAIRS - 1 else ring[:, (2 * p + 1) % 4, :]
                return a, ring[:, (2 * p) % 4, :], c

            def pair_out(t, g):
                h, p = divmod(g, PAIRS)
                state_a, state_m, _ = states(g)
                o = tok_b[:, 2 * P:3 * P]
                pe.wait_ge(a_masked.sem, a_masked.after(t, g))
                pe.matmul(o, a_t[:, :], v_rtok[:, :], start=True, stop=False, skip_group_check=True)
                pe.matmul(o[0:64, :], q_dec[:, chunk(2 * p)], state_a, start=False, stop=False, skip_group_check=True)
                pe.matmul(o[64:128, :], q_dec[:, chunk(2 * p + 1)], state_m, start=False, stop=True,
                          skip_group_check=True).then_inc(o_done.sem, 1)

            def pair_turn(t, g):
                pe.wait_ge(state_c.sem, state_c.after(t, g))
                pe.wait_ge(o_normed.sem, o_normed.after(t, g))
                pe.transpose(pair_b[:, 3 * P:4 * P], o_tok[:, :], ident).then_inc(o_turned.sem, 1)

            def between(t, w, m):
                g = w - PAIR0
                c = w - SCORES0
                if m == 0 and 1 <= g <= G:
                    pair_out(t, g - 1)
                if m == 4:
                    if 0 <= c < CHUNKS:
                        scores(t, c)
                    if 1 <= c <= CHUNKS:
                        turn(t, c - 1)
                    if w == XSUM:
                        sum_x(t + 1)
                if m == 8:
                    if 1 <= g <= G:
                        pair_turn(t, g - 1)
                    if 0 <= g < G:
                        pair_to_tok(t, g)
                if m == 12 and 1 <= c <= CHUNKS:
                    weigh(t, c - 1)
                if m == 16 and 0 <= g < G:
                    pair_products(t, g)

            pe.wait_ge(stored[1], 32)
            pe.wait_ge(dve_setup, 1)
            for k in range(0, KT, 2):
                pe.wait_ge(sq_added, k // 2 + 1)
                mm = pe.matmul(probs_b[:, :], ones[:, :], q_gate[:, k, :], start=(k == 0), stop=(k == KT - 2))
            mm.then_inc(x_summed.sem, 1)
            with pe.Fori(0, TILES) as t:
                for w in range(OUT0):
                    pe.wait_ge(lo_split.sem, lo_split.after(t, w))
                    pe.wait_ge(tile_read.sem, tile_read.after(t, acc_before(w)))
                    for m in range(3 * KT):
                        if w == 0 and m % 3 == 0:
                            pe.wait_ge(h_lo_done.sem, h_lo_done.after(t, m // 3))
                        between(t, w, m)
                        products(w, m, m == 3 * KT - 1)
                pe.wait_ge(mixa_lo.sem, mixa_lo.after(t, QT - 1))
                for w in range(OUT0, OUT0 + 4):
                    pe.wait_ge(lo_split.sem, lo_split.after(t, w))
                    pe.wait_ge(tile_read.sem, tile_read.after(t, acc_before(w)))
                    for m in range(3 * (KT - 1)):
                        if w == OUT0 and m == 3 * (KT - 2):
                            pe.wait_ge(mixh_lo.sem, mixh_lo.after(t, HEADS - 2))
                        between(t, w, m)
                        products(w, m, False)
                pe.wait_ge(mixh_lo.sem, mixh_lo.after(t, HEADS - 1))
                for w in range(OUT0, OUT0 + 4):
                    for m in range(3 * (KT - 1), 3 * KT):
                        products(w, m, m == 3 * KT - 1)
                for w in range(OUT0 + 4, WT):
                    pe.wait_ge(lo_split.sem, lo_split.after(t, w))
                    pe.wait_ge(tile_read.sem, tile_read.after(t, acc_before(w)))
                    for m in range(3 * KT):
                        products(w, m, m == 3 * KT - 1)
                pe.wait_ge(y_added.sem, y_added.after(t, KT - 3))
                pe.matmul(att_b[:, :], ones[:, :], f_c[:, :], start=True, stop=False)
                pe.wait_ge(y_squared.sem, y_squared.after(t, KT - 1))
                pe.matmul(att_b[:, :], ones[:, :], f_d[:, :], start=False, stop=True).then_inc(y_summed.sem, 1)

        @block.scalar
        def _(act):
            for c in (hi_split, gate_ln, gate_sig, f_ln, f_sig, f_log, f_exp, f_end, p_exp, p_turned, kv_ready,
                      o_normed, mixa_hi, mixh_hi, x_squared, h_hi_done, y_squared, x_rstd, y_rstd, act_step):
                c.start(act)
            act.dma_start(vec[:, 2 * KT:], vectors[:, 2 * KT:]).then_inc(stored[0], 16)
            act.dma_start(vec[:, 0:2 * KT], vectors[:, 0:2 * KT]).then_inc(stored[0], 16)
            for i in range(2):
                act.dma_start(sq_in[:, i, :], squares[:, i * P:(i + 1) * P]).then_inc(stored[1], 16)
            act.preload_act_table_set("natural_log_exp_and_others")
            links = [0]

            def then(tile, instruction):
                instruction.then_inc(act_step.sem, 1)
                act.wait_ge(act_step.sem, act_step.after(tile, links[0]))
                links[0] += 1

            def split_hi(tile, w):
                act.wait_ge(tile_done.sem, tile_done.after(tile, before(w, SPLIT_SLOT)))
                wait_weights(act, tile, w)
                act.activation(w_hi[:, SPLIT_SLOT[w], :, :], w_raw[:, RAW_SLOT[w], :, :], ACT.Copy).then_inc(hi_split.sem, 1)

            def log1p_exp(tile, src, dst):
                then(tile, act.activation(dst, src, ACT.Abs))
                then(tile, act.activation(dst, dst, ACT.Exp, scale=-1.0))
                return act.activation(dst, dst, ACT.Ln, bias=1.0)

            def gate_first(t, w, i):
                act.wait_ge(tile_done.sem, tile_done.after(t, w))
                if i == QT:
                    act.wait_ge(tile_read.sem, tile_read.after(t, Z0 + QT - 1))
                elif i:
                    act.wait_ge(tile_read.sem, tile_read.after(t, Z0 + i - 1 if i < QT else gate(i - QT - 1)))
                log1p_exp(t, acc(w)[:, :], g_a[:, :]).then_inc(gate_ln.sem, 1)

            def gate_second(t, i):
                act.wait_ge(gate_arg.sem, gate_arg.after(t, i))
                act.activation(g_a[:, :], g_a[:, :], ACT.Exp).then_inc(gate_sig.sem, 1)

            def rstd(tile, src, dst, width):
                then(tile, act.activation(dst, src, ACT.Ln, scale=1.0 / width, bias=eps[:, :]))
                return act.activation(dst, dst, ACT.Exp, scale=-0.5)

            def square_x(tile, k):
                if k == 0:
                    act.wait_ge(x_loaded, tile * 16)
                else:
                    act.wait_ge(x_added.sem, x_added.after(tile, k - 2))
                dst = x_acc if k == 0 else x_sq
                act.activation(dst[:, :], x_in[:, k, :], ACT.Square).then_inc(x_squared.sem, 1)

            def round_h(tile, k):
                act.wait_ge(h_scaled.sem, h_scaled.after(tile, k))
                act.activation(h_hi[:, k, :], x_in[:, k, :], ACT.Copy).then_inc(h_hi_done.sem, 1)

            def square_y(t, n):
                dst = f_c if n == 0 else (g_a, f_d)[n % 2]
                act.wait_ge(tile_done.sem, tile_done.after(t, OUT0 + n))
                if n >= 3:
                    act.wait_ge(y_added.sem, y_added.after(t, n - 3))
                act.activation(dst[:, :], acc(OUT0 + n)[:, :], ACT.Square).then_inc(y_squared.sem, 1)

            act.wait_ge(dve_setup, 2)
            act.activation(lb_e[:, :], lb_e[:, :], ACT.Exp).then_inc(act_setup, 1)
            for k in range(KT):
                act.wait_ge(x_first[k], 16)
                act.activation(q_gate[:, k, :], x_in[:, k, :], ACT.Square).then_inc(x_squared.sem, 1)
            for w in range(AHEAD):
                split_hi(0, w)
            act.wait_ge(x_summed.sem, x_summed.after(0, 0))
            act.activation(x_acc[:, :], probs_b[:, :], ACT.Ln, scale=1.0 / D_MODEL, bias=eps[:, :]).then_inc(act_setup, 1)
            act.wait_ge(act_setup, 2)
            act.activation(x_acc[:, :], x_acc[:, :], ACT.Exp, scale=-0.5).then_inc(x_rstd.sem, 1)
            for k in range(KT):
                round_h(0, k)

            with act.Fori(0, TILES) as t:
                for s in range(WT):
                    g, c = s - PAIR0, s - SCORES0
                    h, kind = divmod(s - 1 - H0, 4) if H0 < s <= OUT0 else (0, None)
                    z = s - 1 - Z0 if 0 <= s - 1 - Z0 < QT else None
                    if 1 <= g <= G:
                        o = tok_b[:, 2 * P:3 * P]
                        act.wait_ge(o_done.sem, o_done.after(t, g - 1))
                        act.wait_ge(o_turned.sem, o_turned.after(t, g - 2))
                        then(t, act.activation(o_tok[:, :], o, ACT.Square, accum_out=o_sq[:, :]))
                        then(t, rstd(t, o_sq[:, :], o_sq[:, :], P))
                        act.activation(o_tok[:, :], o, ACT.Copy, scale=o_sq[:, :]).then_inc(o_normed.sem, 1)
                    for k in H_PARTS.get(s, ()):
                        round_h(t + 1, k)
                    if s - 1 in ROPE_TILES:
                        r = ROPE_TILES.index(s - 1)
                        src, dst = ((f_a, f_b), (f_c, f_d))[r % 2]
                        act.wait_ge(tile_read.sem, tile_read.after(t, s - 1))
                        for b in range(4):
                            act.dma_start(dst[32 * b:32 * b + 32, :],
                                          src[32 * (b ^ 1):32 * (b ^ 1) + 32, :]).then_inc(swapped[r % 2], 16)
                    if z is not None:
                        gate_first(t, s - 1, z)
                    if kind == 0:
                        act.wait_ge(tile_done.sem, tile_done.after(t, forget(h)))
                        act.wait_ge(k_dec_done.sem, k_dec_done.after(t, h - 1))
                        act.wait_ge(roped.sem, roped.after(t, QT))
                        log1p_exp(t, acc(forget(h))[:, :], f_a[:, :]).then_inc(f_ln.sem, 1)
                    if kind == 1:
                        act.wait_ge(f_scan.sem, f_scan.after(t, h))
                        act.activation(f_d[:, :], f_c[:, :], ACT.Exp)
                        act.activation(f_b[:, :], f_c[:, :], ACT.Exp, scale=-1.0).then_inc(f_exp.sem, 1)
                    if kind == 3:
                        gate_first(t, gate(h), QT + h)
                    if 1 <= c <= CHUNKS:
                        act.wait_ge(turned.sem, turned.after(t, c - 1))
                        act.activation(v_tok[:, :], att_b[:, 2 * P:3 * P], ACT.Copy)
                        act.activation(probs_t[:, :], probs_b[:, :], ACT.Copy).then_inc(p_turned.sem, 1)
                    if 0 <= g < G:
                        act.wait_ge(to_tok.sem, to_tok.after(t, g))
                        act.activation(v_rtok[:, :], tok_b[:, P:2 * P], ACT.Copy)
                        act.activation(k_tok[0:64, 0, :], tok_b[0:64, 0:P], ACT.Copy)
                        act.activation(k_tok[64:128, 1, :], tok_b[64:128, 0:P], ACT.Copy).then_inc(kv_ready.sem, 1)
                    if z is not None:
                        gate_second(t, z)
                    if kind == 0:
                        act.wait_ge(tile_read.sem, tile_read.after(t, forget(h)))
                        act.activation(f_a[:, :], f_a[:, :], ACT.Exp).then_inc(f_sig.sem, 1)
                    if kind == 3:
                        gate_second(t, QT + h)
                    if 1 <= g <= G and g % PAIRS == 0:
                        head = g // PAIRS - 1
                        act.wait_ge(head_mixed.sem, head_mixed.after(t, head))
                        act.activation(mix_hi[:, QT + head, :], h_mix[:, :], ACT.Copy).then_inc(mixh_hi.sem, 1)
                    if s + AHEAD <= OUT0 + 4:
                        split_hi(t, s + AHEAD)
                    if 0 <= c < CHUNKS:
                        act.wait_ge(m_sub.sem, m_sub.after(t, c))
                        act.activation(sink_d[:, :], sink_d[:, :], ACT.Exp, scale=SCALE)
                        act.activation(probs[:, c % 2, :, :], probs[:, c % 2, :, :], ACT.Exp, scale=SCALE).then_inc(p_exp.sem, 1)
                    if kind == 0:
                        act.wait_ge(f_gate.sem, f_gate.after(t, h))
                        act.activation(f_b[:, :], f_b[:, :], ACT.Ln).then_inc(f_log.sem, 1)
                    if kind == 1:
                        act.wait_ge(f_rel.sem, f_rel.after(t, h))
                        act.activation(decay[:, h % 2, :], g_last[:, :], ACT.Exp)
                        act.activation(f_c[:, :], f_c[:, :], ACT.Exp).then_inc(f_end.sem, 1)
                    j = s - (SCORES0 + CHUNKS + 1)
                    if 0 <= j < QT:
                        act.wait_ge(gated.sem, gated.after(t, CHUNKS - 1))
                        act.activation(mix_hi[:, j, :], q_gate[:, QT + j, :], ACT.Copy).then_inc(mixa_hi.sem, 1)
                    if 0 <= s - XSQ0 < KT:
                        square_x(t + 1, s - XSQ0)
                    if s == XSUM:
                        act.wait_ge(x_summed.sem, x_summed.after(t + 1, 0))
                        rstd(t, probs_b[:, :], x_acc[:, :], D_MODEL).then_inc(x_rstd.sem, 1)
                    if s == OUT0 + 3:
                        for n in range(4):
                            square_y(t, n)
                            if n < 3:
                                split_hi(t, OUT0 + 5 + n)
                    if s > OUT0 + 4:
                        square_y(t, s - 1 - OUT0)
                        split_hi(t + 1, s - (WT - AHEAD))
                square_y(t, KT - 1)
                act.wait_ge(y_summed.sem, y_summed.after(t, 0))
                rstd(t, att_b[:, :], g_a[:, :], D_MODEL).then_inc(y_rstd.sem, 1)
                for n in range(0, KT, 2):
                    act.wait_ge(y_done.sem, y_done.after(t, sum(i <= n + 1 for i in Y_DVE) - 1))
                    act.wait_ge(y_pool_done.sem, y_pool_done.after(t, sum(i <= n + 1 for i in Y_POOL) - 1))
                    act.dma_start(out[bass.ts(t, P), n * N:(n + 2) * N].rearrange("p (k n) -> p k n", n=N),
                                  q_gate[:, n:n + 2, :]).then_inc(stored[n // QT], 16)
            assert links[0] == act_step.per_tile, links[0]

        @block.vector
        def _(dve):
            for c in (tile_read, roped, gate_arg, f_gate, f_scan, f_rel, a_masked, state_b, state_c, mixed,
                      head_mixed, m_sub, p_inv, gated, h_scaled, h_lo_done, y_done, dve_step):
                c.start(dve)
            links = [0]

            def then(tile, instruction):
                instruction.then_inc(dve_step.sem, 1)
                dve.wait_ge(dve_step.sem, dve_step.after(tile, links[0]))
                links[0] += 1

            def scale_h(tile, k):
                if k == 0:
                    dve.wait_ge(x_rstd.sem, x_rstd.after(tile, 0))
                dve.scalar_tensor_tensor(x_in[:, k, :], x_in[:, k, :], w_pre[:, k:k + 1], x_acc[:, :],
                                         ALU.mult, ALU.mult).then_inc(h_scaled.sem, 1)

            def low_h(tile, k, parts=1):
                dve.wait_ge(h_hi_done.sem, h_hi_done.after(tile, k))
                dve.tensor_tensor(h_lo[:, k, :], x_in[:, k, :], h_hi[:, k, :], ALU.subtract).then_inc(h_lo_done.sem, parts)

            dve.memset(ones[:, :], 1.0).then_inc(dve_setup, 1)
            dve.memset(eps[:, :], EPS)
            dve.memset(carry[:, :, :], 0.0)
            dve.memset(k_t[:, :, :], 0.0)
            dve.memset(k_tok[:, :, :], 0.0)
            dve.memset(v_t[:, 0:CHUNK], 0.0)
            dve.memset(a_t[:, :], 0.0)
            dve.memset(first_mask[:, 0:CHUNK], NEG_INF)
            dve.memset(first_mask[:, CHUNK:P], 0.0)
            dve.memset(reset[:, :].rearrange("p (c n) -> p c n", n=CHUNK)[:, :, 1:CHUNK], 1.0)
            dve.memset(reset[:, :].rearrange("p (c n) -> p c n", n=CHUNK)[:, :, 0:1], 0.0)
            dve.wait_ge(stored[0], 32)
            dve.wait_ge(stored[1], 32)
            dve.tensor_tensor(lb_m[:, :], lb_in[:, 0:HEADS], lb_in[:, HEADS:], ALU.max).then_inc(lb_step, 1)
            dve.wait_ge(lb_step, 1)
            dve.tensor_tensor(lb_e[:, 0:HEADS], lb_in[:, 0:HEADS], lb_m[:, :], ALU.subtract)
            dve.tensor_tensor(lb_e[:, HEADS:], lb_in[:, HEADS:], lb_m[:, :], ALU.subtract).then_inc(dve_setup, 1)
            dve.wait_ge(act_setup, 1)
            dve.tensor_tensor(lb_m[:, :], lb_e[:, 0:HEADS], lb_e[:, HEADS:], ALU.add).then_inc(lb_step, 1)
            dve.wait_ge(lb_step, 2)
            dve.reciprocal(lb_m[:, :], lb_m[:, :]).then_inc(lb_step, 1)
            dve.wait_ge(lb_step, 3)
            dve.tensor_tensor(lb[:, :], lb_e[:, 0:HEADS], lb_m[:, :], ALU.mult).then_inc(lb_step, 1)
            dve.wait_ge(lb_step, 4)
            dve.tensor_scalar(lb_rest[:, :], lb[:, :], -1.0, 1.0, ALU.mult, ALU.add)
            dve.tensor_scalar(sink8[:, :], sink_in, 1.0 / SCALE, None, ALU.mult)
            for k in range(0, KT, 2):
                dve.wait_ge(x_squared.sem, x_squared.after(0, k + 1))
                dve.tensor_tensor(q_gate[:, k, :], q_gate[:, k, :], q_gate[:, k + 1, :], ALU.add).then_inc(sq_added, 1)
            for k in range(0, KT + 2, 2):
                if k < KT:
                    scale_h(0, k)
                    scale_h(0, k + 1)
                if k:
                    dve.wait_ge(first_low, k // 2)
                    low_h(0, k - 1, 2)

            def per_chunk(ap):
                return ap.rearrange("p (c n) -> p c n", n=CHUNK)

            def rope_copy(t, r):
                w = ROPE_TILES[r]
                src = (f_a, f_c)[r % 2]
                dve.wait_ge(tile_done.sem, tile_done.after(t, w))
                dve.wait_ge(k_dec_done.sem, k_dec_done.after(t, -1))
                dve.wait_ge(roped.sem, roped.after(t, r - 2))
                dve.tensor_copy(src[:, :], acc(w)[:, :]).then_inc(tile_read.sem, 1)

            def rope_turn(t, r):
                a, b = ((f_a, f_b), (f_c, f_d))[r % 2]
                if r == 0:
                    dve.wait_ge(tables_loaded, t * 32 + 32)
                dve.wait_ge(*loaded(swapped[r % 2], (3, 2)[r % 2], t, r // 2, 4))
                dve.tensor_tensor(a[:, :], a[:, :], cos_t[:, :], ALU.mult)
                then(t, dve.tensor_tensor(b[:, :], b[:, :], sin_t[:, :], ALU.mult))
                if r == 0:
                    for g in range(2):
                        rows = slice(64 * g, 64 * g + 64)
                        last = dve.tensor_tensor(k_t[rows, g, CHUNK:], a[rows, :], b[rows, :], ALU.add)
                else:
                    dve.wait_ge(stored[0], t * 32 + 32)
                    last = dve.tensor_tensor(queries[:, (r - 1) // 2, :, (r - 1) % 2, :], per_chunk(a[:, :]),
                                             per_chunk(b[:, :]), ALU.add)
                last.then_inc(roped.sem, 1)

            def gate_first(t, w, i):
                dve.wait_ge(gate_ln.sem, gate_ln.after(t, i))
                dve.scalar_tensor_tensor(g_a[:, :], acc(w)[:, :], 0.0, g_a[:, :], ALU.min, ALU.subtract).then_inc(gate_arg.sem, 1)

            def gate_second(t, w, i, dst):
                dve.wait_ge(gate_sig.sem, gate_sig.after(t, i))
                dve.tensor_tensor(dst, acc(w)[:, :], g_a[:, :], ALU.mult).then_inc(tile_read.sem, 1)

            def mix_pair(t, g):
                h, p = divmod(g, PAIRS)
                dve.wait_ge(o_turned.sem, o_turned.after(t, g))
                if p == 0:
                    dve.wait_ge(mixh_lo.sem, mixh_lo.after(t, h - 1))
                dve.tensor_scalar(h_mix[:, pair(p)], pair_b[:, 3 * P:4 * P], w_head, None, ALU.mult).then_inc(mixed.sem, 1)
                if p == PAIRS - 1:
                    dve.wait_ge(mixed.sem, mixed.after(t, g))
                    dve.tensor_tensor(h_mix[:, :], h_mix[:, :], z_r[:, :], ALU.mult).then_inc(head_mixed.sem, 1)

            def copy_y(t, n):
                dve.wait_ge(y_squared.sem, y_squared.after(t, n))
                dve.tensor_scalar(q_gate[:, n, :], acc(OUT0 + n)[:, :], w_post[:, n:n + 1], None, ALU.mult).then_inc(tile_read.sem, 1)

            with dve.Fori(0, TILES) as t:
                for s in range(WT):
                    g, c = s - PAIR0, s - SCORES0
                    h_of, kind = divmod(s - 1 - H0, 4) if H0 < s <= OUT0 else (0, None)
                    if s - 1 in ROPE_TILES:
                        rope_copy(t, ROPE_TILES.index(s - 1))
                    if s - 1 == V_TILE:
                        dve.wait_ge(tile_done.sem, tile_done.after(t, V_TILE))
                        dve.tensor_copy(v_t[:, CHUNK:], acc(V_TILE)[:, :]).then_inc(tile_read.sem, 1)
                    if kind == 2:
                        dve.wait_ge(tile_done.sem, tile_done.after(t, query(h_of)))
                        dve.wait_ge(o_done.sem, o_done.after(t, PAIRS * h_of - 1))
                        dve.tensor_tensor(q_dec[:, :], acc(query(h_of))[:, :], f_d[:, :], ALU.mult).then_inc(tile_read.sem, 1)
                        dve.wait_ge(tile_done.sem, tile_done.after(t, value(h_of)))
                        dve.tensor_copy(v_r[:, :], acc(value(h_of))[:, :]).then_inc(tile_read.sem, 1)
                    for k in H_PARTS.get(s, ()):
                        scale_h(t + 1, k)
                    if 1 <= g <= G and c >= CHUNKS:
                        mix_pair(t, g - 1)
                    if g == G:
                        dve.wait_ge(mixh_hi.sem, mixh_hi.after(t, HEADS - 1))
                        dve.tensor_tensor(mix_lo[:, KT - 1, :], h_mix[:, :], mix_hi[:, KT - 1, :], ALU.subtract).then_inc(mixh_lo.sem, 1)
                    for k in H_PARTS.get(s, ()):
                        low_h(t + 1, k)
                    if s - 2 in ROPE_TILES:
                        rope_turn(t, ROPE_TILES.index(s - 2))
                    if 0 <= s - 1 - Z0 < QT:
                        gate_first(t, s - 1, s - 1 - Z0)
                    if kind == 0:
                        dve.wait_ge(f_ln.sem, f_ln.after(t, h_of))
                        dve.scalar_tensor_tensor(f_a[:, :], acc(forget(h_of))[:, :], 0.0, f_a[:, :], ALU.min,
                                                 ALU.subtract).then_inc(tile_read.sem, 1)
                    if kind == 1:
                        dve.wait_ge(f_exp.sem, f_exp.after(t, h_of))
                        then(t, dve.tensor_copy(g_last[:, :], per_chunk(f_c[:, :])[:, :, CHUNK - 1]))
                        dve.tensor_tensor(per_chunk(f_c[:, :]), g_last[:, :].unsqueeze(2).broadcast_to([P, CHUNKS, CHUNK]),
                                          per_chunk(f_c[:, :]), ALU.subtract).then_inc(f_rel.sem, 1)
                    if kind == 3:
                        gate_first(t, gate(h_of), QT + h_of)
                    if 0 <= c < CHUNKS:
                        pr = probs[:, c % 2, :, :]
                        src = score_b[:, :].rearrange("p (b m) -> p b m", b=4)
                        dve.wait_ge(scored.sem, scored.after(t, c))
                        if c == 0:
                            then(t, dve.tensor_tensor(pr, src, first_mask[:, :].unsqueeze(1).broadcast_to([P, 4, P]), ALU.add))
                            src = pr
                        then(t, dve.reduce_max(top[:, :], src, axis=AX.X))
                        then(t, dve.tensor_tensor(s_max[:, :], top[:, :], sink8[:, :], ALU.max))
                        dve.tensor_tensor(sink_d[:, :], sink8[:, :], s_max[:, :], ALU.subtract)
                        dve.tensor_tensor(pr, src, s_max[:, :].unsqueeze(2).broadcast_to([P, 4, P]), ALU.subtract).then_inc(m_sub.sem, 1)
                        if c == 0:
                            dve.memset(first_mask[:, 0:CHUNK], 0.0)
                    if 1 <= g <= G and c < CHUNKS:
                        mix_pair(t, g - 1)
                    if 0 <= s - 1 - Z0 < QT:
                        dve.wait_ge(stored[1], t * 32 + 32)
                        gate_second(t, s - 1, s - 1 - Z0, q_gate[:, s - 1 - Z0 + QT, :])
                    if kind == 0:
                        dve.wait_ge(f_sig.sem, f_sig.after(t, h_of))
                        then(t, dve.tensor_scalar(f_b[:, :], f_a[:, :], lb_rest[:, h_of:h_of + 1], lb[:, h_of:h_of + 1],
                                                  ALU.mult, ALU.add))
                        dve.tensor_scalar(f_a[:, :], f_b[:, :], -1.0, 1.0, ALU.mult, ALU.add).then_inc(f_gate.sem, 1)
                    if 0 <= g < G:
                        h, p = divmod(g, PAIRS)
                        a = carry[:, h, :] if p == 0 else ring[:, (2 * p + 3) % 4, :]
                        m = ring[:, (2 * p) % 4, :]
                        z = carry[:, h, :] if p == PAIRS - 1 else ring[:, (2 * p + 1) % 4, :]
                        dve.wait_ge(a_u.sem, a_u.after(t, g))
                        dve.scalar_tensor_tensor(m, a, decay[:, h % 2, 2 * p:2 * p + 1], pair_b[:, P:2 * P],
                                                 ALU.mult, ALU.add).then_inc(state_b.sem, 1)
                        dve.copy_predicated(a_t[:, :], causal, pair_b[:, 0:P]).then_inc(a_masked.sem, 1)
                        dve.wait_ge(state_b.sem, state_b.after(t, g))
                        dve.scalar_tensor_tensor(z, m, decay[:, h % 2, 2 * p + 1:2 * p + 2], pair_b[:, 2 * P:3 * P],
                                                 ALU.mult, ALU.add).then_inc(state_c.sem, 1)
                    if 0 <= c < CHUNKS:
                        dve.wait_ge(p_exp.sem, p_exp.after(t, c))
                        dve.wait_ge(p_normed.sem, p_normed.after(t, c - 1))
                        then(t, dve.reduce_sum(s_sum[:, :], probs[:, c % 2, :, :], axis=AX.X))
                        then(t, dve.tensor_tensor(s_sum[:, :], s_sum[:, :], sink_d[:, :], ALU.add))
                        dve.reciprocal(s_inv[:, :], s_sum[:, :]).then_inc(p_inv.sem, 1)
                    if 1 <= c <= CHUNKS:
                        gates = q_gate[:, QT:, chunk(c - 1)]
                        dve.wait_ge(weighed.sem, weighed.after(t, c - 1))
                        if c == 1:
                            dve.wait_ge(tile_read.sem, tile_read.after(t, Z0 + QT - 1))
                        dve.tensor_tensor(gates, att_b[:, 0:2 * P].rearrange("p (j n) -> p j n", j=QT), gates,
                                          ALU.mult).then_inc(gated.sem, 1)
                        if c == CHUNKS:
                            dve.tensor_copy(k_t[:, :, 0:CHUNK], k_t[:, :, N:])
                            dve.tensor_copy(v_t[:, 0:CHUNK], v_t[:, N:])
                    if kind == 0:
                        dve.wait_ge(f_log.sem, f_log.after(t, h_of))
                        dve.tensor_tensor_scan(f_c[:, :], reset[:, :], f_b[:, :], 0.0, ALU.mult, ALU.add).then_inc(f_scan.sem, 1)
                    if kind == 3:
                        gate_second(t, gate(h_of), QT + h_of, z_r[:, :])
                    if s == OUT0 + 3:
                        for n in range(4):
                            copy_y(t, n)
                    if s > OUT0 + 4:
                        copy_y(t, s - 1 - OUT0)
                copy_y(t, KT - 1)
                dve.wait_ge(tile_read.sem, tile_read.after(t, WT - 1))
                dve.wait_ge(y_rstd.sem, y_rstd.after(t, 0))
                dve.wait_ge(res_loaded, t * 32 + 32)
                for i in range(0, len(Y_DVE), 2):
                    tiles = Y_DVE[i:i + 2]
                    for n in tiles:
                        mult = dve.tensor_tensor(q_gate[:, n, :], q_gate[:, n, :], g_a[:, :], ALU.mult)
                    then(t, mult)
                    for n in tiles:
                        dve.tensor_tensor(q_gate[:, n, :], q_gate[:, n, :], x_in[:, n, :], ALU.add).then_inc(y_done.sem, 1)
            assert links[0] == dve_step.per_tile, links[0]

        @block.gpsimd
        def _(pool):
            for c in (lo_split, k_dec_done, k_end_done, p_normed, mixa_lo, mixh_lo, x_added, y_added,
                      y_scaled, y_pool_done):
                c.start(pool)
            x_added.start(pool)
            def split_lo(tile, w):
                pool.wait_ge(hi_split.sem, hi_split.after(tile, w))
                s = SPLIT_SLOT[w]
                pool.tensor_tensor(w_lo[:, s, :, :], w_raw[:, RAW_SLOT[w], :, :], w_hi[:, s, :, :], ALU.subtract).then_inc(lo_split.sem, 1)

            def add_x(tile, k):
                pool.wait_ge(x_squared.sem, x_squared.after(tile, k))
                pool.wait_ge(x_added.sem, x_added.after(tile, k - 2))
                pool.tensor_tensor(x_acc[:, :], x_acc[:, :], x_sq[:, :], ALU.add).then_inc(x_added.sem, 1)

            def add_y(t, n):
                pool.wait_ge(y_squared.sem, y_squared.after(t, n))
                pool.wait_ge(y_added.sem, y_added.after(t, n - 2))
                pool.tensor_tensor(f_c[:, :], f_c[:, :], (g_a, f_d)[n % 2][:, :], ALU.add).then_inc(y_added.sem, 1)

            split_lo(0, 0)
            split_lo(0, 1)
            for k in range(0, KT, 2):
                pool.wait_ge(h_hi_done.sem, h_hi_done.after(0, k))
                pool.tensor_tensor(h_lo[:, k, :], x_in[:, k, :], h_hi[:, k, :], ALU.subtract).then_inc(first_low, 1)
            for w in range(2, AHEAD):
                split_lo(0, w)
            with pool.Fori(0, TILES) as t:
                for s in range(WT):
                    g, c = s - PAIR0, s - SCORES0
                    h_of, kind = divmod(s - 1 - H0, 4) if H0 < s <= OUT0 else (0, None)
                    if kind == 2:
                        pool.wait_ge(f_exp.sem, f_exp.after(t, h_of))
                        pool.wait_ge(a_u.sem, a_u.after(t, PAIRS * h_of - 1))
                        pool.tensor_tensor(k_dec[:, :], f_a[:, :], f_b[:, :], ALU.mult).then_inc(k_dec_done.sem, 1)
                    j = s - 1 - (SCORES0 + CHUNKS + 1)
                    if 0 <= j < QT:
                        pool.wait_ge(mixa_hi.sem, mixa_hi.after(t, j))
                        pool.tensor_tensor(mix_lo[:, j, :], q_gate[:, QT + j, :], mix_hi[:, j, :], ALU.subtract).then_inc(mixa_lo.sem, 1)
                    if 0 < s - 1 - XSQ0 < KT:
                        add_x(t + 1, s - 1 - XSQ0)
                    if 1 <= g < G and g % PAIRS == 0:
                        h = g // PAIRS - 1
                        pool.wait_ge(mixh_hi.sem, mixh_hi.after(t, h))
                        pool.tensor_tensor(mix_lo[:, QT + h, :], h_mix[:, :], mix_hi[:, QT + h, :],
                                           ALU.subtract).then_inc(mixh_lo.sem, 1)
                    if s + AHEAD <= OUT0 + 4:
                        split_lo(t, s + AHEAD)
                    if 0 <= c < CHUNKS:
                        pr = probs[:, c % 2, :, :]
                        pool.wait_ge(p_inv.sem, p_inv.after(t, c))
                        pool.tensor_tensor(pr, pr, s_inv[:, :].unsqueeze(2).broadcast_to([P, 4, P]), ALU.mult).then_inc(p_normed.sem, 1)
                    if kind == 1:
                        pool.wait_ge(f_end.sem, f_end.after(t, h_of))
                        pool.wait_ge(to_tok.sem, to_tok.after(t, PAIRS * h_of - 1))
                        pool.tensor_tensor(k_end[:, :], f_a[:, :], f_c[:, :], ALU.mult).then_inc(k_end_done.sem, 1)
                    if s == OUT0 + 3:
                        for n in range(1, 4):
                            split_lo(t, OUT0 + 4 + n)
                            add_y(t, n)
                    if s > OUT0 + 4:
                        add_y(t, s - 1 - OUT0)
                        split_lo(t + 1, s - (WT - AHEAD))
                for i, n in enumerate(Y_POOL):
                    y = q_gate[:, n, :]
                    pool.wait_ge(y_rstd.sem, y_rstd.after(t, 0))
                    pool.wait_ge(tile_read.sem, tile_read.after(t, OUT0 + n))
                    pool.tensor_tensor(y, y, g_a[:, :], ALU.mult).then_inc(y_scaled.sem, 1)
                    pool.wait_ge(res_loaded, t * 32 + 32)
                    pool.wait_ge(y_scaled.sem, y_scaled.after(t, i))
                    pool.tensor_tensor(y, y, x_in[:, n, :], ALU.add).then_inc(y_pool_done.sem, 1)


def weight_tiles(w_in, w_out):
    head = lambda start, j: slice(start + 64 * j, start + 64 * j + 64)
    starts = np.cumsum([0, 512, 128, 128, 512, 512, 512, 512])
    q_a, k_a, v_a, z_a, q_r, f_r, i_r, z_r = (int(v) for v in starts)
    columns = [w_in[:, k_a:k_a + P], w_in[:, v_a:v_a + P]]
    for start in (q_a, z_a):
        columns += [w_in[:, head(start, j + QT * g)] for j in range(QT) for g in range(2)]
    for h in range(HEADS):
        columns += [w_in[:, start + P * h:start + P * (h + 1)] for start in (f_r, q_r, i_r, z_r)]
    columns = np.concatenate(columns, axis=1).reshape(KT, P, OUT0, P).transpose(2, 1, 0, 3)
    rows = [w_out[head(0, j + QT * g)] for j in range(QT) for g in range(2)] + [w_out[512:]]
    rows = np.concatenate(rows, axis=0).reshape(KT, P, KT, P).transpose(2, 1, 0, 3)
    return np.concatenate([columns, rows], axis=0).reshape(WT * P, KT * P)


def rope_tables():
    half = 32
    inv = np.float32(ROPE_THETA) ** (-np.arange(half, dtype=np.float32) / np.float32(half))
    angle = inv[:, None] * np.arange(SEQ, dtype=np.float32)[None, :]
    cos, sin = np.cos(angle), np.sin(angle)
    cos, sin = np.concatenate([cos] * 4, axis=0), np.concatenate([-sin, sin, -sin, sin], axis=0)
    tiled = lambda a: np.ascontiguousarray(a.reshape(P, TILES, N).transpose(1, 0, 2).reshape(TILES * P, N), dtype=np.float32)
    return tiled(cos), tiled(sin)


def kernel(x, w_norm_pre, w_in, attn_sinks, hgrn_lb, hgrn_norm, w_out, w_norm_post):
    import concourse.bacc as bacc
    from concourse.bass_utils import run_bass_kernel_spmd

    x = np.asarray(x)
    by_tile = x[0].reshape(TILES, N, KT, P).transpose(0, 3, 2, 1).reshape(TILES * P, KT * N)
    cos, sin = rope_tables()
    by_partition = lambda v: np.asarray(v).reshape(-1, P).T
    sinks = np.repeat(np.asarray(attn_sinks)[0].reshape(2, 2, 2).transpose(2, 0, 1).reshape(2, 4), CHUNK, axis=0)
    vectors = np.concatenate([by_partition(w_norm_pre), by_partition(w_norm_post), by_partition(hgrn_norm),
                              by_partition(hgrn_lb), sinks], axis=1)
    m, l = np.arange(P)[:, None], np.arange(P)[None, :]
    squares = np.concatenate([np.eye(P), (m // CHUNK == l // CHUNK) & (l >= m)], axis=1).astype(np.float32)
    arrays = {
        "x": by_tile, "weights": weight_tiles(np.asarray(w_in)[0], np.asarray(w_out)[0]),
        "cos": cos, "sin": sin, "vectors": vectors, "squares": squares,
    }
    arrays = {f"in_{name}": np.ascontiguousarray(a) for name, a in arrays.items()}

    nc = bacc.Bacc("TRN2", target_bir_lowering=False, num_devices=1)
    aps = [nc.dram_tensor(name, a.shape, FP32, kind="ExternalInput").ap() for name, a in arrays.items()]
    out = nc.dram_tensor("out", by_tile.shape, FP32, kind="ExternalOutput").ap()
    hybrid_block(nc, *aps, out)
    got = run_bass_kernel_spmd(nc, [arrays], core_ids=[0]).results[0]["out"]
    return got.reshape(TILES, P, KT, N).transpose(0, 3, 2, 1).reshape(1, SEQ, D_MODEL)
```

```python
import math
from contextlib import ExitStack

import numpy as np
import concourse.bass as bass
from concourse import mybir

FP32 = mybir.dt.float32
FP32R = mybir.dt.float32r
INT32 = mybir.dt.int32
ALU = mybir.AluOpType
ACT = mybir.ActivationFunctionType
AX = mybir.AxisListType

P = 128
SEQ, D_MODEL = 2048, 1024
N = 512
TILES = SEQ // N
KT = D_MODEL // P
CHUNK = 64
CHUNKS = N // CHUNK
PAIRS = N // P
HEADS = 4
QT = 4
EPS = 1e-6
NEG_INF = -1e30
SCALE = 0.125
ROPE_THETA = 10000.0

K_TILE, V_TILE = 0, 1
Q0, Z0 = 2, 2 + QT
H0 = Z0 + QT
OUT0 = H0 + 4 * HEADS
WT = OUT0 + KT
ROPE_TILES = [K_TILE] + [Q0 + j for j in range(QT)]
RAW_SLOTS = 4
RAW_SLOT = [w % RAW_SLOTS for w in range(WT)]
SPLIT_SLOT = [s for r in (4, 4, 4, 4, 4, 4, 4, 3, 3) for s in range(r)]
RAW_USES = [RAW_SLOT.count(s) for s in range(RAW_SLOTS)]
assert len(SPLIT_SLOT) == WT and OUT0 == 26

SCORES0 = Z0 + 3
PAIR0 = H0 + 3
XSQ = [s for s in range(PAIR0 + 3, OUT0) if (s - 1 - H0) % 4 != 0][:KT]
MIXA = {SCORES0 + CHUNKS + 3: (0, 1), SCORES0 + CHUNKS + 4: (2, 3)}
H_PARTS = {OUT0 + 1: (0, 1, 2), OUT0 + 2: (3, 4, 5), OUT0 + 3: (6, 7)}
XSUM = 2


def forget(h):
    return H0 + 4 * h


def query(h):
    return H0 + 4 * h + 1


def value(h):
    return H0 + 4 * h + 2


def gate(h):
    return H0 + 4 * h + 3


def before(w, slot):
    return next(v for v in range(w - 1, w - WT - 1, -1) if slot[v % WT] == slot[w])


def split_at(s):
    return [w for w in (s + 2, s + 3) if w - s == (2 if w % WT in (0, 1, 2, 31, 32, 33) else 3)]


FIRST_SPLIT = 2
FIRST_SQUARES = (0, 2, 4, 6, 1, 3)
FIRST_POOL = 3


Y_POOL = (0, 2)


class Count:

    def __init__(self, sem, per_tile):
        self.sem, self.per_tile = sem, per_tile

    def start(self, engine):
        engine.sem_inc(self.sem, self.per_tile)

    def after(self, tile, i):
        assert -self.per_tile <= i < self.per_tile
        return tile * self.per_tile + (self.per_tile + i + 1)


def hybrid_block(nc, x, x_rows, weights, cos, sin, vectors, w_post, squares, out):
    ctx = ExitStack()
    with ctx:
        def sb(name, shape, dt=FP32):
            return ctx.enter_context(nc.sbuf_tensor(name, [P] + shape, dt))

        def sem(name):
            return ctx.enter_context(nc.semaphore(name))

        x_in = sb("x_in", [KT, N])
        h_hi, h_lo = sb("h_hi", [KT, N], FP32R), sb("h_lo", [KT, N], FP32R)
        mix_hi, mix_lo = sb("mix_hi", [KT, N], FP32R), sb("mix_lo", [KT, N], FP32R)
        w_raw = sb("w_raw", [RAW_SLOTS, KT, P])
        w_hi, w_lo = (sb(n, [max(SPLIT_SLOT) + 1, KT, P], FP32R) for n in ("w_hi", "w_lo"))
        q_gate = sb("q_gate", [2 * QT, N])
        queries = q_gate[:, 0:QT, :].rearrange("p q n -> p (q n)").rearrange(
            "p (h c j n) -> p h c j n", h=2, c=CHUNKS, j=2)
        k_t = sb("k_t", [2, CHUNK + N])
        v_t = sb("v_t", [CHUNK + N])
        cos_t, sin_t = sb("cos_t", [N]), sb("sin_t", [N])
        f_a, f_b, f_c, f_d = (sb(f"f_{c}", [N]) for c in "abcd")
        g_a, g_b = sb("g_a", [N]), sb("g_b", [N])
        q_dec = sb("q_dec", [PAIRS, 3, CHUNK])
        k_end = sb("k_end", [PAIRS, 3, CHUNK])
        k_dec = sb("k_dec", [N])
        v_r, z_r, h_mix = sb("v_r", [N]), sb("z_r", [N]), sb("h_mix", [N])
        probs = sb("probs", [2, 4, P])
        probs_t = sb("probs_t", [N])
        v_tok = sb("v_tok", [P])
        kv_tok = sb("kv_tok", [2, P])
        a_t = sb("a_t", [P])
        o_tok = sb("o_tok", [P])
        carry = sb("carry", [HEADS, P])
        ring = sb("ring", [2, P])
        x_sq, x_acc, x_scale = sb("x_sq", [N]), sb("x_acc", [N]), sb("x_scale", [N])
        reset = sb("reset", [N])
        ones = sb("ones", [P])
        sq_in = sb("sq_in", [2, P])
        ident = sq_in[:, 0, :]
        causal = sq_in[:, 1, :].bitcast(INT32)
        first_mask = sb("first_mask", [P])
        w_post_t = sb("w_post_t", [2, N])
        vec = sb("vec", [KT + 1 + 2 * HEADS + 4])
        w_pre, w_head = vec[:, 0:KT], vec[:, KT:KT + 1]
        lb_in, sink_in = vec[:, KT + 1:KT + 1 + 2 * HEADS], vec[:, KT + 1 + 2 * HEADS:]
        lb, lb_rest = sb("lb", [HEADS]), sb("lb_rest", [HEADS])
        lb_e = sb("lb_e", [2 * HEADS])
        lb_m = sb("lb_m", [HEADS])
        sink8 = sb("sink8", [4])
        g_last = sb("g_last", [CHUNKS])
        decay, pair_decay = sb("decay", [2, CHUNKS]), sb("pair_decay", [2, PAIRS])
        top, s_max, s_sum, s_inv = (sb(n, [4]) for n in ("top", "s_max", "s_sum", "s_inv"))
        sink_d = sb("sink_d", [4])
        o_sq = sb("o_sq", [1])
        y_sq, y_bias, y_scale = sb("y_sq", [8]), sb("y_bias", [4]), sb("y_scale", [4])
        eps = sb("eps", [1])

        bank = [ctx.enter_context(nc.psum_tensor(f"bank{i}", [P, N], FP32)) for i in range(8)]
        score_b, probs_b, att_b, tok_b, pair_b = bank[3:]

        def acc(w):
            return bank[w % 3]

        y_bank = (score_b, bank[2], bank[0], bank[1]), (probs_b, att_b, tok_b, pair_b)

        x_first = [sem(f"x_first{k}") for k in range(0, KT, 2)]
        x_loaded, tables_loaded = sem("x_loaded"), sem("tables_loaded")
        w_loaded = [sem(f"w_loaded{i}") for i in range(RAW_SLOTS)]
        swapped = [sem(f"swapped{i}") for i in range(2)]
        res_loaded = sem("res_loaded")
        stored = [sem(f"stored{i}") for i in range(2)]

        def count(name, per_tile):
            return Count(sem(name), per_tile)

        tile_done = count("tile_done", WT - 2)
        x_summed, y_done = count("x_summed", 1), count("y_done", 8)
        scored, turned, weighed = (count(n, CHUNKS) for n in ("scored", "turned", "weighed"))
        G = HEADS * PAIRS
        to_tok, a_u, o_done, o_turned = (count(n, G) for n in ("to_tok", "a_u", "o_done", "o_turned"))
        hi_split = count("hi_split", WT)
        gate_ln, gate_sig = (count(n, QT + HEADS) for n in ("gate_ln", "gate_sig"))
        f_ln, f_sig, f_log, f_exp, f_end = (count(n, HEADS) for n in ("f_ln", "f_sig", "f_log", "f_exp", "f_end"))
        p_exp, p_turned = count("p_exp", CHUNKS), count("p_turned", CHUNKS)
        kv_ready, o_normed = count("kv_ready", G), count("o_normed", G)
        mixa_hi, mixh_hi = count("mixa_hi", QT), count("mixh_hi", HEADS)
        x_squared, h_hi_done = count("x_squared", KT), count("h_hi_done", KT)
        y_squared, x_rstd, y_rstd = count("y_squared", 8), count("x_rstd", 1), count("y_rstd", 4)
        act_step = count("act_step", 2 * (QT + HEADS) + 2 * HEADS + 3 * HEADS * PAIRS + 1 + 4)
        tile_read = count("tile_read", OUT0)
        roped = count("roped", len(ROPE_TILES))
        gate_arg = count("gate_arg", QT + HEADS)
        f_gate, f_scan, f_rel = (count(n, HEADS) for n in ("f_gate", "f_scan", "f_rel"))
        a_masked, state_done, mixed = (count(n, G) for n in ("a_masked", "state_done", "mixed"))
        head_mixed = count("head_mixed", HEADS)
        m_sub, p_inv, gated = (count(n, CHUNKS) for n in ("m_sub", "p_inv", "gated"))
        h_lo_done = count("h_lo_done", KT)
        gate_done = count("gate_done", QT + HEADS)
        f_arg, f_d_scaled = count("f_arg", HEADS), count("f_d_scaled", HEADS)
        y_read, y_biased, finished = count("y_read", 8), count("y_biased", 1), count("finished", 8 - len(Y_POOL))
        dve_step = count("dve_step", 1 + len(ROPE_TILES) + CHUNKS * 4 + 1 + HEADS * 2)
        dve_setup, lb_step = sem("dve_setup"), sem("lb_step")
        act_setup, sum_step, vec_loaded = sem("act_setup"), sem("sum_step"), sem("vec_loaded")
        lo_split = count("lo_split", WT)
        k_dec_done, k_chunk_end, k_end_done = (count(n, HEADS) for n in ("k_dec_done", "k_chunk_end", "k_end_done"))
        p_normed = count("p_normed", CHUNKS)
        mixa_lo, mixh_lo = count("mixa_lo", QT), count("mixh_lo", HEADS)
        x_added = count("x_added", KT - 1)
        y_scaled, finished_pool = count("y_scaled", 2), count("finished_pool", 2)
        pool_sum = sem("pool_sum")

        def loaded(sems, uses, tile, i, n=1):
            return (sems, tile * (16 * n * uses) + 16 * n * (i + 1))

        def wait_weights(engine, tile, w):
            engine.wait_ge(*loaded(w_loaded[RAW_SLOT[w]], RAW_USES[RAW_SLOT[w]], tile, w // RAW_SLOTS))

        def chunk(c, n=1):
            return slice(c * CHUNK, (c + n) * CHUNK)

        def by_pair(ap):
            return ap.rearrange("p (q c n) -> p q c n", q=PAIRS, c=2)

        def decays(h, i):
            d = decay[:, h % 2, :].rearrange("p (q c) -> p q c", c=2)[:, :, i]
            return d.unsqueeze(2).broadcast_to([P, PAIRS, CHUNK])

        def states(g):
            h, p = divmod(g, PAIRS)
            return (carry[:, h, :] if p == 0 else ring[:, (p - 1) % 2, :],
                    carry[:, h, :] if p == PAIRS - 1 else ring[:, p % 2, :])

        def pair(p):
            return slice(p * P, (p + 1) * P)

        block = ctx.enter_context(nc.Block())

        @block.sync
        def _(sp):
            def load_x(tile, row):
                sp.wait_ge(h_lo_done.sem, h_lo_done.after(tile, -1))
                sp.wait_ge(x_squared.sem, x_squared.after(tile, -1))
                sp.wait_ge(finished.sem, finished.after(tile - 1, -1))
                sp.wait_ge(finished_pool.sem, finished_pool.after(tile - 1, -1))
                sp.dma_start(x_in[:, :, :], x[bass.ts(row, P), :].rearrange("p (k n) -> p k n", k=KT)).then_inc(x_loaded, 16)

            def load_weights(tile, w):
                sp.wait_ge(lo_split.sem, lo_split.after(tile, before(w, RAW_SLOT)))
                sp.dma_start(w_raw[:, RAW_SLOT[w], :, :],
                             weights[w * P:(w + 1) * P, :].rearrange("p (k m) -> p k m", k=KT)).then_inc(w_loaded[RAW_SLOT[w]], 16)

            def load_residual(t, half):
                k = half * KT // 2
                sp.wait_ge(h_lo_done.sem, h_lo_done.after(t + 1, k + KT // 2 - 1))
                sp.dma_start(x_in[:, k:k + KT // 2, :].rearrange("p (b h) n -> p b (h n)", h=2),
                             x_rows[bass.ds(t * N + half * 2 * P, 2 * P), :].rearrange("(b p) f -> p b f", p=P)).then_inc(res_loaded, 16)

            for w in range(FIRST_SPLIT):
                load_weights(0, w)
            for k in range(0, KT, 2):
                sp.dma_start(x_in[:, k:k + 2, :], x[0:P, k * N:(k + 2) * N].rearrange("p (k n) -> p k n", n=N)).then_inc(x_first[k // 2], 16)
            with sp.Fori(0, TILES) as t:
                for v in range(WT):
                    w = (v + FIRST_SPLIT) % WT
                    load_weights(t + (v + FIRST_SPLIT) // WT, w)
                    if v == 2:
                        sp.wait_ge(roped.sem, roped.after(t, -1))
                        sp.dma_start(cos_t[:, :], cos[bass.ts(t, P), :]).then_inc(tables_loaded, 16)
                        sp.dma_start(sin_t[:, :], sin[bass.ts(t, P), :]).then_inc(tables_loaded, 16)
                    if w == H0:
                        load_x(t + 1, (t + 1) % TILES)
                    if w == WT - 3:
                        load_residual(t, 0)
                    if w == WT - 1:
                        load_residual(t, 1)
            for w in range(FIRST_SPLIT):
                wait_weights(sp, TILES, w)
            sp.wait_ge(stored[0], 32 * (TILES + 1))
            sp.wait_ge(stored[1], 48 * TILES + 32)

        @block.tensor
        def _(pe):
            for c in (tile_done, x_summed, y_done, scored, turned, weighed, to_tok, a_u, o_done, o_turned):
                c.start(pe)

            def sum_x(tile):
                pe.wait_ge(y_read.sem, y_read.after(tile, -4))
                pe.wait_ge(x_added.sem, x_added.after(tile, KT - 2))
                pe.matmul(probs_b[:, :], ones[:, :], x_acc[:, :], start=True, stop=True).then_inc(x_summed.sem, 1)

            def products(w, m, last):
                k, part = m // 3, m % 3
                s = SPLIT_SLOT[w]
                stationary, moving = ((w_hi, h_hi), (w_lo, h_hi), (w_hi, h_lo))[part]
                mm = pe.matmul(acc(w)[:, :], stationary[:, s, k, :], moving[:, k, :],
                               start=(m == 0), stop=(m == 3 * KT - 1), skip_group_check=True)
                if last:
                    mm.then_inc(tile_done.sem, 1)

            def out_product(half, k, b, part):
                w = OUT0 + 4 * half + k // 2
                mix, weight = ((mix_hi, w_hi), (mix_lo, w_hi), (mix_hi, w_lo))[part]
                mm = pe.matmul(y_bank[half][b][:, :], mix[:, k, b * P:(b + 1) * P],
                               weight[:, SPLIT_SLOT[w], (k % 2) * 4:(k % 2) * 4 + 4, :].rearrange("p a m -> p (a m)"),
                               start=(k == 0 and part == 0), stop=(k == KT - 1 and part == 2), skip_group_check=True)
                if k == KT - 1 and part == 2:
                    mm.then_inc(y_done.sem, 1)
                return mm

            def scores(t, c):
                if c == 0:
                    pe.wait_ge(roped.sem, roped.after(t, QT))
                    pe.wait_ge(y_read.sem, y_read.after(t, -1))
                else:
                    pe.wait_ge(m_sub.sem, m_sub.after(t, c - 1))
                for b in range(4):
                    g, hp = b // 2, b % 2
                    mm = pe.matmul(score_b[:, pair(b)], queries[:, hp, c, :, :].rearrange("p j n -> p (j n)"),
                                   k_t[:, g, chunk(c, 2)], start=True, stop=True)
                mm.then_inc(scored.sem, 1)

            def turn(t, c):
                pe.wait_ge(gated.sem, gated.after(t, c - 1))
                pe.transpose(att_b[:, 2 * P:3 * P], v_t[:, chunk(c, 2)], ident)
                pe.wait_ge(p_normed.sem, p_normed.after(t, c))
                for b in range(4):
                    mm = pe.transpose(probs_b[:, pair(b)], probs[:, c % 2, b, :], ident)
                mm.then_inc(turned.sem, 1)

            def weigh(t, c):
                pe.wait_ge(p_turned.sem, p_turned.after(t, c))
                for g in range(2):
                    mm = pe.matmul(att_b[64 * g:64 * g + 64, 0:2 * P], v_tok[:, 64 * g:64 * g + 64],
                                   probs_t[:, 2 * P * g:2 * P * (g + 1)], start=True, stop=True)
                mm.then_inc(weighed.sem, 1)

            def pair_to_tok(t, g):
                h, p = divmod(g, PAIRS)
                if p == 0:
                    pe.wait_ge(k_end_done.sem, k_end_done.after(t, h))
                    pe.wait_ge(tile_read.sem, tile_read.after(t, value(h)))
                pe.transpose(tok_b[:, 0:P], k_end[:, p, 1:3, :].rearrange("p c n -> p (c n)"), ident)
                pe.transpose(tok_b[:, P:2 * P], v_r[:, pair(p)], ident).then_inc(to_tok.sem, 1)

            def pair_products(t, g):
                h, p = divmod(g, PAIRS)
                if p == 0:
                    pe.wait_ge(k_dec_done.sem, k_dec_done.after(t, h))
                pe.wait_ge(mixed.sem, mixed.after(t, g - 1))
                pe.wait_ge(kv_ready.sem, kv_ready.after(t, g))
                pe.matmul(pair_b[:, 0:P].rearrange("p (c n) -> p c n", c=2), k_dec[:, pair(p)], q_dec[:, p, 0::2, :],
                          start=True, stop=True)
                pe.matmul(pair_b[0:CHUNK, CHUNK:P], k_end[:, p, 0, :], q_dec[:, p, 2, :], start=True, stop=True)
                pe.matmul(pair_b[:, P:2 * P], kv_tok[:, 0, :], kv_tok[:, 1, :], start=True, stop=True).then_inc(a_u.sem, 1)

            def pair_out(t, g):
                o = tok_b[:, 2 * P:3 * P]
                pe.wait_ge(a_masked.sem, a_masked.after(t, g))
                pe.matmul(o, a_t[:, :], kv_tok[:, 1, :], start=True, stop=False, skip_group_check=True)
                pe.matmul(o, q_dec[:, g % PAIRS, 0:2, :].rearrange("p c n -> p (c n)"), states(g)[0],
                          start=False, stop=True, skip_group_check=True).then_inc(o_done.sem, 1)

            def pair_turn(t, g):
                pe.wait_ge(state_done.sem, state_done.after(t, g))
                pe.wait_ge(o_normed.sem, o_normed.after(t, g))
                pe.transpose(pair_b[:, 3 * P:4 * P], o_tok[:, :], ident).then_inc(o_turned.sem, 1)

            def between(t, w, m):
                g = w - PAIR0
                c = w - SCORES0
                if m == 0 and 1 <= g <= G:
                    pair_out(t, g - 1)
                if m == 0 and w == XSUM:
                    pe.wait_ge(stored[1], 32)
                if m == 4:
                    if 0 <= c < CHUNKS:
                        scores(t, c)
                    if 1 <= c <= CHUNKS:
                        turn(t, c - 1)
                if m == 8:
                    if 1 <= g <= G:
                        pair_turn(t, g - 1)
                    if 0 <= g < G:
                        pair_to_tok(t, g)
                if m == 12 and 1 <= c <= CHUNKS:
                    weigh(t, c - 1)
                if m == 0 and w == XSUM:
                    sum_x(t)
                if m == 16 and 0 <= g < G:
                    pair_products(t, g)

            pe.wait_ge(dve_setup, 1)
            for i in range(4):
                pe.matmul(tok_b[:, :], ones[:, :], reset[:, :], start=True, stop=True)
            with pe.Fori(0, TILES) as t:
                for w in range(OUT0):
                    pe.wait_ge(lo_split.sem, lo_split.after(t, w))
                    if w < 3:
                        pe.wait_ge(y_read.sem, y_read.after(t, (2, 3, 1)[w] - 8))
                    else:
                        pe.wait_ge(tile_read.sem, tile_read.after(t, w - 3))
                    for m in range(3 * KT):
                        if w == 0 and m % 3 == 0:
                            pe.wait_ge(h_lo_done.sem, h_lo_done.after(t, m // 3))
                        between(t, w, m)
                        products(w, m, m == 3 * KT - 1)
                pe.wait_ge(mixa_lo.sem, mixa_lo.after(t, QT - 1))
                order = [(2 * w + i, b) for w in range(3) for b in range(4) for i in range(2)] + [(KT - 2, b) for b in range(4)]
                step = 3 * (KT - 1)
                for i, (k, b) in enumerate(order):
                    for part in range(3):
                        between(t, OUT0 + (3 * i + part) // step, (3 * i + part) % step)
                        if part == 0 and i % 8 == 0:
                            pe.wait_ge(lo_split.sem, lo_split.after(t, OUT0 + i // 8))
                        if part == 0 and k == 0 and b:
                            pe.wait_ge(tile_read.sem, tile_read.after(t, OUT0 - 4 + b))
                        if part == 0 and i % 8 == 0 and k == KT - 2:
                            pe.wait_ge(mixh_lo.sem, mixh_lo.after(t, HEADS - 2))
                        mm = out_product(0, k, b, part)
                    if i % 8 == 7:
                        mm.then_inc(tile_done.sem, 1)
                pe.wait_ge(mixh_lo.sem, mixh_lo.after(t, HEADS - 1))
                for b in range(4):
                    for part in range(3):
                        mm = out_product(0, KT - 1, b, part)
                for w in range(4):
                    pe.wait_ge(lo_split.sem, lo_split.after(t, OUT0 + 4 + w))
                    for b in range(4):
                        for k in (2 * w, 2 * w + 1):
                            for part in range(3):
                                mm = out_product(1, k, b, part)
                    if w < 3:
                        mm.then_inc(tile_done.sem, 1)

        @block.scalar
        def _(act):
            for c in (hi_split, gate_ln, gate_sig, f_ln, f_sig, f_log, f_exp, f_end, p_exp, p_turned, kv_ready,
                      o_normed, mixa_hi, mixh_hi, x_squared, h_hi_done, y_squared, x_rstd, y_rstd, act_step):
                c.start(act)
            act.dma_start(vec[:, :], vectors).then_inc(vec_loaded, 16)
            act.preload_act_table_set("natural_log_exp_and_others")
            for i in range(2):
                act.dma_start(sq_in[:, i, :], squares[:, i * P:(i + 1) * P]).then_inc(stored[1], 16)
            links = [0]

            def then(tile, instruction):
                instruction.then_inc(act_step.sem, 1)
                act.wait_ge(act_step.sem, act_step.after(tile, links[0]))
                links[0] += 1

            def split_hi(tile, w):
                v = before(w, SPLIT_SLOT)
                if v % WT in (OUT0 + 3, WT - 1):
                    act.wait_ge(y_done.sem, y_done.after(tile, (3 if v % WT == OUT0 + 3 else 7) - (8 if v < 0 else 0)))
                else:
                    place = v % WT - (v % WT > OUT0 + 3)
                    act.wait_ge(tile_done.sem, tile_done.after(tile, place - (tile_done.per_tile if v < 0 else 0)))
                wait_weights(act, tile, w)
                act.activation(w_hi[:, SPLIT_SLOT[w], :, :], w_raw[:, RAW_SLOT[w], :, :], ACT.Copy).then_inc(hi_split.sem, 1)

            def log1p_exp(tile, src, dst):
                then(tile, act.activation(dst, src, ACT.Abs))
                then(tile, act.activation(dst, dst, ACT.Exp, scale=-1.0))
                return act.activation(dst, dst, ACT.Ln, bias=1.0)

            def gate_first(t, i):
                act.wait_ge(tile_read.sem, tile_read.after(t, Z0 + i if i < QT else gate(i - QT)))
                act.wait_ge(gate_done.sem, gate_done.after(t, i - 1))
                log1p_exp(t, g_b[:, :], g_a[:, :]).then_inc(gate_ln.sem, 1)

            def gate_second(t, i):
                act.wait_ge(gate_arg.sem, gate_arg.after(t, i))
                act.activation(g_a[:, :], g_a[:, :], ACT.Exp).then_inc(gate_sig.sem, 1)

            def exp_scores(t, c):
                act.wait_ge(m_sub.sem, m_sub.after(t, c))
                act.activation(sink_d[:, :], sink_d[:, :], ACT.Exp, scale=SCALE)
                act.activation(probs[:, c % 2, :, :], probs[:, c % 2, :, :], ACT.Exp, scale=SCALE).then_inc(p_exp.sem, 1)

            def rstd(tile, src, dst, width, bias=eps[:, :]):
                then(tile, act.activation(dst, src, ACT.Ln, scale=1.0 / width, bias=bias))
                return act.activation(dst, dst, ACT.Exp, scale=-0.5)

            def square_x(tile, k):
                if k == 0:
                    act.wait_ge(x_loaded, tile * 16)
                else:
                    act.wait_ge(x_added.sem, x_added.after(tile, k - 2))
                dst = x_acc if k == 0 else x_sq
                act.activation(dst[:, :], x_in[:, k, :], ACT.Square).then_inc(x_squared.sem, 1)

            def round_h(tile, k):
                act.activation(h_hi[:, k, :], x_in[:, k, :], ACT.Copy, scale=w_pre[:, k:k + 1]).then_inc(h_hi_done.sem, 1)

            def square_y(t, half, b):
                i = 4 * half + b
                act.wait_ge(y_done.sem, y_done.after(t, i))
                act.wait_ge(y_squared.sem, y_squared.after(t, i - 1))
                act.activation(f_c[:, :], y_bank[half][b][:, :], ACT.Square, accum_out=y_sq[:, i:i + 1]).then_inc(y_squared.sem, 1)

            split_hi(0, 0)
            act.wait_ge(vec_loaded, 16)

            for k in range(0, KT, 2):
                act.wait_ge(x_first[k // 2], 16)
                round_h(0, k)
                round_h(0, k + 1)
                if k == 0:
                    for w in range(1, FIRST_SPLIT):
                        split_hi(0, w)
            for i, k in enumerate(FIRST_SQUARES):
                steps = KT - i if i == len(FIRST_SQUARES) - 1 else 1
                act.activation(q_gate[:, k, :], x_in[:, k, :], ACT.Square).then_inc(x_squared.sem, steps)
            for h in range(2):
                act.dma_start(w_post_t[:, h, :], w_post[:, h * N:(h + 1) * N]).then_inc(stored[0], 16)
            act.wait_ge(dve_setup, 2)
            act.activation(lb_e[:, :], lb_e[:, :], ACT.Exp).then_inc(act_setup, 1)

            with act.Fori(0, TILES) as t:
                for s in range(WT):
                    g, c = s - PAIR0, s - SCORES0
                    h, kind = divmod(s - 1 - H0, 4) if H0 < s <= OUT0 else (0, None)
                    z = s - 1 - Z0 if 0 <= s - 1 - Z0 < QT else None
                    if s == XSUM:
                        act.wait_ge(x_summed.sem, x_summed.after(t, 0))
                        rstd(t, probs_b[:, :], x_scale[:, :], D_MODEL).then_inc(x_rstd.sem, 1)
                    if 1 <= g <= G:
                        o = tok_b[:, 2 * P:3 * P]
                        act.wait_ge(o_done.sem, o_done.after(t, g - 1))
                        act.wait_ge(o_turned.sem, o_turned.after(t, g - 2))
                        then(t, act.activation(o_tok[:, :], o, ACT.Square, accum_out=o_sq[:, :]))
                        then(t, rstd(t, o_sq[:, :], o_sq[:, :], P))
                        act.activation(o_tok[:, :], o, ACT.Copy, scale=o_sq[:, :]).then_inc(o_normed.sem, 1)
                    for k in H_PARTS.get(s, ()):
                        round_h(t + 1, k)
                    if s == K_TILE + 1:
                        for w in split_at(s):
                            split_hi(t + w // WT, w % WT)
                    if s - 1 in ROPE_TILES:
                        r = ROPE_TILES.index(s - 1)
                        src, dst = ((f_a, f_b), (f_c, f_d))[r % 2]
                        act.wait_ge(tile_read.sem, tile_read.after(t, s - 1))
                        for b in range(4):
                            act.dma_start(dst[32 * b:32 * b + 32, :],
                                          src[32 * (b ^ 1):32 * (b ^ 1) + 32, :]).then_inc(swapped[r % 2], 16)
                    if z is not None:
                        gate_first(t, z)
                    if kind == 0:
                        act.wait_ge(tile_read.sem, tile_read.after(t, forget(h)))
                        log1p_exp(t, f_b[:, :], f_a[:, :]).then_inc(f_ln.sem, 1)
                    if kind == 1:
                        act.wait_ge(f_scan.sem, f_scan.after(t, h))
                        act.activation(f_d[:, :], f_c[:, :], ACT.Exp)
                        act.activation(f_b[:, :], f_c[:, :], ACT.Exp, scale=-1.0).then_inc(f_exp.sem, 1)
                    if kind == 3:
                        gate_first(t, QT + h)
                    if 1 <= c <= CHUNKS:
                        act.wait_ge(turned.sem, turned.after(t, c - 1))
                        act.activation(v_tok[:, :], att_b[:, 2 * P:3 * P], ACT.Copy)
                        act.activation(probs_t[:, :], probs_b[:, :], ACT.Copy).then_inc(p_turned.sem, 1)
                    if 0 <= g < G:
                        act.wait_ge(to_tok.sem, to_tok.after(t, g))
                        act.activation(kv_tok[:, :, :], tok_b[:, 0:2 * P], ACT.Copy).then_inc(kv_ready.sem, 1)
                    if 0 <= c < 3:
                        exp_scores(t, c)
                    if z is not None:
                        gate_second(t, z)
                    if kind == 0:
                        act.wait_ge(f_arg.sem, f_arg.after(t, h))
                        act.activation(f_a[:, :], f_a[:, :], ACT.Exp).then_inc(f_sig.sem, 1)
                    if kind == 3:
                        gate_second(t, QT + h)
                    if 1 <= g <= G and g % PAIRS == 0:
                        head = g // PAIRS - 1
                        act.wait_ge(head_mixed.sem, head_mixed.after(t, head))
                        act.activation(mix_hi[:, QT + head, :], h_mix[:, :], ACT.Copy).then_inc(mixh_hi.sem, 1)
                    for w in split_at(s) if s != K_TILE + 1 else ():
                        split_hi(t + w // WT, w % WT)
                    if 3 <= c < CHUNKS:
                        exp_scores(t, c)
                    if kind == 0:
                        act.wait_ge(f_gate.sem, f_gate.after(t, h))
                        act.activation(f_b[:, :], f_b[:, :], ACT.Ln).then_inc(f_log.sem, 1)
                    if kind == 1:
                        act.wait_ge(f_rel.sem, f_rel.after(t, h))
                        act.activation(decay[:, h % 2, :], g_last[:, :], ACT.Exp)
                        act.activation(f_c[:, :], f_c[:, :], ACT.Exp).then_inc(f_end.sem, 1)
                    for j in MIXA.get(s, ()):
                        act.wait_ge(gated.sem, gated.after(t, CHUNKS - 1))
                        act.activation(mix_hi[:, j, :], q_gate[:, QT + j, :], ACT.Copy).then_inc(mixa_hi.sem, 1)
                    if s in XSQ:
                        square_x(t + 1, XSQ.index(s))
                    if s == OUT0 + 4:
                        for b in range(4):
                            square_y(t, 0, b)
                for b in range(4):
                    square_y(t, 1, b)
                    if b == 0:
                        act.wait_ge(y_biased.sem, y_biased.after(t, 0))
                    act.wait_ge(y_squared.sem, y_squared.after(t, 4 + b))
                    rstd(t, y_sq[:, 4 + b:5 + b], y_scale[:, b:b + 1], D_MODEL, y_bias[:, b:b + 1]).then_inc(y_rstd.sem, 1)
                for b, cols in ((0, (0, 1)), (1, (0, 1)), (2, (0, 1)), (3, (0,)), (3, (1,))):
                    pieces = sum(2 - (i in Y_POOL) for i in range(b)) + cols[-1] + 1 - (b in Y_POOL)
                    act.wait_ge(finished.sem, finished.after(t, pieces - 1))
                    if b in Y_POOL:
                        act.wait_ge(finished_pool.sem, finished_pool.after(t, b // 2))
                    act.dma_start(out[bass.ds(t * N + b * P, P), cols[0] * N:(cols[-1] + 1) * N].rearrange("p (h n) -> p h n", n=N),
                                  q_gate[:, 2 * b + cols[0]:2 * b + cols[-1] + 1, :]).then_inc(stored[b // 2], 16)
            assert links[0] == act_step.per_tile, links[0]

        @block.vector
        def _(dve):
            for c in (tile_read, roped, gate_arg, f_gate, f_scan, f_rel, a_masked, state_done, mixed,
                      head_mixed, m_sub, p_inv, gated, gate_done, f_arg, f_d_scaled, h_lo_done, y_read, y_biased, finished, dve_step):
                c.start(dve)
            links = [0]

            def then(tile, instruction):
                instruction.then_inc(dve_step.sem, 1)
                dve.wait_ge(dve_step.sem, dve_step.after(tile, links[0]))
                links[0] += 1

            def low_h(tile, k):
                dve.wait_ge(h_hi_done.sem, h_hi_done.after(tile, k))
                dve.scalar_tensor_tensor(h_lo[:, k, :], x_in[:, k, :], w_pre[:, k:k + 1], h_hi[:, k, :],
                                         ALU.mult, ALU.subtract).then_inc(h_lo_done.sem, 1)

            dve.memset(ones[:, :], 1.0)
            dve.memset(reset[:, :].rearrange("p (c n) -> p c n", n=CHUNK)[:, :, 1:CHUNK], 1.0)
            dve.memset(reset[:, :].rearrange("p (c n) -> p c n", n=CHUNK)[:, :, 0:1], 0.0).then_inc(dve_setup, 1)
            dve.memset(eps[:, :], EPS)
            dve.memset(carry[:, :, :], 0.0)
            dve.memset(k_t[:, :, :], 0.0)
            dve.memset(v_t[:, 0:CHUNK], 0.0)
            dve.memset(a_t[:, :], 0.0)
            dve.memset(first_mask[:, 0:CHUNK], NEG_INF)
            dve.memset(first_mask[:, CHUNK:P], 0.0)
            dve.wait_ge(hi_split.sem, hi_split.after(0, 0))
            dve.tensor_tensor(w_lo[:, 0, :, :], w_raw[:, 0, :, :], w_hi[:, 0, :, :], ALU.subtract).then_inc(lo_split.sem, 1)
            dve.wait_ge(vec_loaded, 16)
            for k in range(KT):
                low_h(0, k)
            dve.tensor_tensor(lb_m[:, :], lb_in[:, 0:HEADS], lb_in[:, HEADS:], ALU.max).then_inc(lb_step, 1)
            dve.wait_ge(lb_step, 1)
            dve.tensor_tensor(lb_e[:, 0:HEADS], lb_in[:, 0:HEADS], lb_m[:, :], ALU.subtract)
            dve.tensor_tensor(lb_e[:, HEADS:], lb_in[:, HEADS:], lb_m[:, :], ALU.subtract).then_inc(dve_setup, 1)
            own = [k for k in range(KT) if k not in FIRST_SQUARES]
            for k in own:
                dve.tensor_tensor(q_gate[:, k, :], x_in[:, k, :], x_in[:, k, :], ALU.mult).then_inc(sum_step, 1)
            terms = [own[1]] + list(FIRST_SQUARES[FIRST_POOL:])
            for i, k in enumerate(terms):
                dve.wait_ge(sum_step, len(own) + i)
                if i:
                    dve.wait_ge(x_squared.sem, x_squared.after(0, FIRST_POOL + i - 1))
                dve.tensor_tensor(x_acc[:, :], x_acc[:, :] if i else q_gate[:, own[0], :], q_gate[:, k, :],
                                  ALU.add).then_inc(sum_step, 1)
            dve.wait_ge(sum_step, len(own) + len(terms))
            dve.wait_ge(pool_sum, FIRST_POOL - 1)
            dve.tensor_tensor(x_acc[:, :], x_acc[:, :], x_sq[:, :], ALU.add).then_inc(x_added.sem, x_added.per_tile)
            dve.wait_ge(act_setup, 1)
            dve.tensor_tensor(lb_m[:, :], lb_e[:, 0:HEADS], lb_e[:, HEADS:], ALU.add).then_inc(lb_step, 1)
            dve.wait_ge(lb_step, 2)
            dve.reciprocal(lb_m[:, :], lb_m[:, :]).then_inc(lb_step, 1)
            dve.wait_ge(lb_step, 3)
            dve.tensor_tensor(lb[:, :], lb_e[:, 0:HEADS], lb_m[:, :], ALU.mult).then_inc(lb_step, 1)
            dve.wait_ge(lb_step, 4)
            dve.tensor_scalar(lb_rest[:, :], lb[:, :], -1.0, 1.0, ALU.mult, ALU.add)
            dve.tensor_scalar(sink8[:, :], sink_in, 1.0 / SCALE, None, ALU.mult)
            dve.wait_ge(stored[1], 32)

            def per_chunk(ap):
                return ap.rearrange("p (c n) -> p c n", n=CHUNK)

            def rope_copy(t, r):
                w = ROPE_TILES[r]
                src = (f_a, f_c)[r % 2]
                dve.wait_ge(tile_done.sem, tile_done.after(t, w))
                dve.wait_ge(k_dec_done.sem, k_dec_done.after(t, -1))
                dve.wait_ge(roped.sem, roped.after(t, r - 2))
                dve.tensor_copy(src[:, :], acc(w)[:, :]).then_inc(tile_read.sem, 1)

            def rope_turn(t, r):
                a, b = ((f_a, f_b), (f_c, f_d))[r % 2]
                if r == 0:
                    dve.wait_ge(tables_loaded, t * 32 + 32)
                    dve.tensor_tensor(cos_t[:, :], cos_t[:, :], x_scale[:, :], ALU.mult)
                    then(t, dve.tensor_tensor(sin_t[:, :], sin_t[:, :], x_scale[:, :], ALU.mult))
                dve.wait_ge(*loaded(swapped[r % 2], (3, 2)[r % 2], t, r // 2, 4))
                dve.tensor_tensor(a[:, :], a[:, :], cos_t[:, :], ALU.mult)
                then(t, dve.tensor_tensor(b[:, :], b[:, :], sin_t[:, :], ALU.mult))
                if r == 0:
                    for g in range(2):
                        rows = slice(64 * g, 64 * g + 64)
                        last = dve.tensor_tensor(k_t[rows, g, CHUNK:], a[rows, :], b[rows, :], ALU.add)
                else:
                    dve.wait_ge(stored[0], t * 32 + 32)
                    last = dve.tensor_tensor(queries[:, (r - 1) // 2, :, (r - 1) % 2, :], per_chunk(a[:, :]),
                                             per_chunk(b[:, :]), ALU.add)
                last.then_inc(roped.sem, 1)

            def gate_scale(t, w, i):
                dve.wait_ge(tile_done.sem, tile_done.after(t, w))
                dve.wait_ge(gate_done.sem, gate_done.after(t, i - 1))
                dve.tensor_tensor(g_b[:, :], acc(w)[:, :], x_scale[:, :], ALU.mult).then_inc(tile_read.sem, 1)

            def gate_first(t, i):
                dve.wait_ge(gate_ln.sem, gate_ln.after(t, i))
                dve.scalar_tensor_tensor(g_a[:, :], g_b[:, :], 0.0, g_a[:, :], ALU.min, ALU.subtract).then_inc(gate_arg.sem, 1)

            def gate_second(t, i, dst):
                dve.wait_ge(gate_sig.sem, gate_sig.after(t, i))
                dve.tensor_tensor(dst, g_b[:, :], g_a[:, :], ALU.mult).then_inc(gate_done.sem, 1)

            def carry_state(t, g):
                h, p = divmod(g, PAIRS)
                state, after = states(g)
                dve.wait_ge(a_u.sem, a_u.after(t, g))
                dve.scalar_tensor_tensor(after, state, pair_decay[:, h % 2, p:p + 1], pair_b[:, P:2 * P],
                                         ALU.mult, ALU.add).then_inc(state_done.sem, 1)
                dve.copy_predicated(a_t[:, :], causal, pair_b[:, 0:P]).then_inc(a_masked.sem, 1)

            def softmax_first(t, c):
                pr = probs[:, c % 2, :, :]
                src = score_b[:, :].rearrange("p (b m) -> p b m", b=4)
                dve.wait_ge(scored.sem, scored.after(t, c))
                if c == 0:
                    then(t, dve.tensor_tensor(pr, src, first_mask[:, :].unsqueeze(1).broadcast_to([P, 4, P]), ALU.add))
                    src = pr
                then(t, dve.reduce_max(top[:, :], src, axis=AX.X))
                then(t, dve.tensor_tensor(s_max[:, :], top[:, :], sink8[:, :], ALU.max))
                dve.tensor_tensor(sink_d[:, :], sink8[:, :], s_max[:, :], ALU.subtract)
                dve.tensor_tensor(pr, src, s_max[:, :].unsqueeze(2).broadcast_to([P, 4, P]), ALU.subtract).then_inc(m_sub.sem, 1)
                if c == 0:
                    dve.memset(first_mask[:, 0:CHUNK], 0.0)

            def softmax_sums(t, c):
                dve.wait_ge(p_exp.sem, p_exp.after(t, c))
                dve.wait_ge(p_normed.sem, p_normed.after(t, c - 1))
                then(t, dve.reduce_sum(s_sum[:, :], probs[:, c % 2, :, :], axis=AX.X))
                then(t, dve.tensor_tensor(s_sum[:, :], s_sum[:, :], sink_d[:, :], ALU.add))
                dve.reciprocal(s_inv[:, :], s_sum[:, :]).then_inc(p_inv.sem, 1)

            def mix_pair(t, g):
                h, p = divmod(g, PAIRS)
                dve.wait_ge(o_turned.sem, o_turned.after(t, g))
                if p == 0:
                    dve.wait_ge(mixh_lo.sem, mixh_lo.after(t, h - 1))
                dve.tensor_scalar(h_mix[:, pair(p)], pair_b[:, 3 * P:4 * P], w_head, None, ALU.mult).then_inc(mixed.sem, 1)
                if p == PAIRS - 1:
                    dve.wait_ge(mixed.sem, mixed.after(t, g))
                    dve.tensor_tensor(h_mix[:, :], h_mix[:, :], z_r[:, :], ALU.mult).then_inc(head_mixed.sem, 1)

            def copy_y(t, half, b):
                dve.wait_ge(y_squared.sem, y_squared.after(t, 4 * half + b))
                dve.tensor_tensor(q_gate[:, 2 * b + half, :], y_bank[half][b][:, :], w_post_t[:, half, :], ALU.mult).then_inc(y_read.sem, 1)

            with dve.Fori(0, TILES) as t:
                for s in range(WT):
                    g, c = s - PAIR0, s - SCORES0
                    h_of, kind = divmod(s - 1 - H0, 4) if H0 < s <= OUT0 else (0, None)
                    if 0 <= s - 1 - Z0 < QT:
                        gate_scale(t, s - 1, s - 1 - Z0)
                    if kind == 3:
                        gate_scale(t, gate(h_of), QT + h_of)
                    if kind == 0:
                        dve.wait_ge(tile_done.sem, tile_done.after(t, forget(h_of)))
                        dve.wait_ge(k_dec_done.sem, k_dec_done.after(t, h_of - 1))
                        dve.wait_ge(roped.sem, roped.after(t, QT))
                        dve.tensor_tensor(f_b[:, :], acc(forget(h_of))[:, :], x_scale[:, :], ALU.mult).then_inc(tile_read.sem, 1)
                    if s - 1 in ROPE_TILES:
                        rope_copy(t, ROPE_TILES.index(s - 1))
                    if s - 1 == V_TILE:
                        dve.wait_ge(tile_done.sem, tile_done.after(t, V_TILE))
                        dve.wait_ge(x_rstd.sem, x_rstd.after(t, 0))
                        dve.tensor_tensor(v_t[:, CHUNK:], acc(V_TILE)[:, :], x_scale[:, :], ALU.mult).then_inc(tile_read.sem, 1)
                    if kind == 2:
                        dve.wait_ge(tile_done.sem, tile_done.after(t, query(h_of)))
                        dve.wait_ge(o_done.sem, o_done.after(t, PAIRS * h_of - 1))
                        dve.wait_ge(f_d_scaled.sem, f_d_scaled.after(t, h_of))
                        dve.tensor_tensor(q_dec[:, :, 0::2, :], by_pair(acc(query(h_of))[:, :]), by_pair(f_d[:, :]),
                                          ALU.mult).then_inc(tile_read.sem, 1)
                        dve.wait_ge(tile_done.sem, tile_done.after(t, value(h_of)))
                        dve.tensor_tensor(v_r[:, :], acc(value(h_of))[:, :], x_scale[:, :], ALU.mult).then_inc(tile_read.sem, 1)
                        dve.wait_ge(f_end.sem, f_end.after(t, h_of))
                        d = decay[:, h_of % 2, :].rearrange("p (q c) -> p q c", c=2)
                        dve.tensor_tensor(pair_decay[:, h_of % 2, :], d[:, :, 0], d[:, :, 1], ALU.mult)
                        dve.wait_ge(tile_read.sem, tile_read.after(t, query(h_of)))
                        dve.tensor_tensor(q_dec[:, :, 1, :], q_dec[:, :, 2, :], decays(h_of, 0), ALU.mult)
                    if 1 <= g <= G and c >= CHUNKS:
                        mix_pair(t, g - 1)
                    if g == G:
                        dve.wait_ge(mixh_hi.sem, mixh_hi.after(t, HEADS - 1))
                        dve.tensor_tensor(mix_lo[:, KT - 1, :], h_mix[:, :], mix_hi[:, KT - 1, :], ALU.subtract).then_inc(mixh_lo.sem, 1)
                    for k in H_PARTS.get(s, ()):
                        low_h(t + 1, k)
                    if s - 2 in ROPE_TILES:
                        rope_turn(t, ROPE_TILES.index(s - 2))
                    if 0 <= c < CHUNKS:
                        softmax_first(t, c)
                    if 0 <= s - 1 - Z0 < QT:
                        gate_first(t, s - 1 - Z0)
                    if kind == 0:
                        dve.wait_ge(f_ln.sem, f_ln.after(t, h_of))
                        dve.scalar_tensor_tensor(f_a[:, :], f_b[:, :], 0.0, f_a[:, :], ALU.min, ALU.subtract).then_inc(f_arg.sem, 1)
                    if kind == 1:
                        dve.wait_ge(f_exp.sem, f_exp.after(t, h_of))
                        then(t, dve.tensor_copy(g_last[:, :], per_chunk(f_c[:, :])[:, :, CHUNK - 1]))
                        dve.tensor_tensor(per_chunk(f_c[:, :]), g_last[:, :].unsqueeze(2).broadcast_to([P, CHUNKS, CHUNK]),
                                          per_chunk(f_c[:, :]), ALU.subtract).then_inc(f_rel.sem, 1)
                        dve.tensor_tensor(f_d[:, :], f_d[:, :], x_scale[:, :], ALU.mult).then_inc(f_d_scaled.sem, 1)
                    if kind == 3:
                        gate_first(t, QT + h_of)
                    if 1 <= g <= G and c < CHUNKS:
                        mix_pair(t, g - 1)
                    if 0 <= c < 3:
                        softmax_sums(t, c)
                    if 0 <= s - 1 - Z0 < QT:
                        dve.wait_ge(stored[1], t * 48 + 32)
                        gate_second(t, s - 1 - Z0, q_gate[:, s - 1 - Z0 + QT, :])
                    if 0 <= g < G and kind == 0:
                        carry_state(t, g)
                    if kind == 0:
                        dve.wait_ge(f_sig.sem, f_sig.after(t, h_of))
                        then(t, dve.tensor_scalar(f_b[:, :], f_a[:, :], lb_rest[:, h_of:h_of + 1], lb[:, h_of:h_of + 1],
                                                  ALU.mult, ALU.add))
                        dve.tensor_scalar(f_a[:, :], f_b[:, :], -1.0, 1.0, ALU.mult, ALU.add).then_inc(f_gate.sem, 1)
                    if kind == 3:
                        gate_second(t, QT + h_of, z_r[:, :])
                    if 0 <= g < G and kind != 0:
                        carry_state(t, g)
                    if 3 <= c < CHUNKS:
                        softmax_sums(t, c)
                    if 1 <= c <= CHUNKS:
                        gates = q_gate[:, QT:, chunk(c - 1)]
                        dve.wait_ge(weighed.sem, weighed.after(t, c - 1))
                        if c == 1:
                            dve.wait_ge(gate_done.sem, gate_done.after(t, QT - 1))
                        dve.tensor_tensor(gates, att_b[:, 0:2 * P].rearrange("p (j n) -> p j n", j=QT), gates,
                                          ALU.mult).then_inc(gated.sem, 1)
                        if c == CHUNKS:
                            dve.tensor_copy(k_t[:, :, 0:CHUNK], k_t[:, :, N:])
                            dve.tensor_copy(v_t[:, 0:CHUNK], v_t[:, N:])
                    if kind == 0:
                        dve.wait_ge(f_log.sem, f_log.after(t, h_of))
                        dve.tensor_tensor_scan(f_c[:, :], reset[:, :], f_b[:, :], 0.0, ALU.mult, ALU.add).then_inc(f_scan.sem, 1)
                    if s == OUT0 + 4:
                        for b in range(4):
                            copy_y(t, 0, b)
                        dve.tensor_scalar(y_bias[:, :], y_sq[:, 0:4], 1.0 / D_MODEL, EPS, ALU.mult, ALU.add).then_inc(y_biased.sem, 1)
                for b in range(4):
                    copy_y(t, 1, b)
                    if b == 0:
                        dve.wait_ge(res_loaded, t * 32 + 32)
                    dve.wait_ge(y_rstd.sem, y_rstd.after(t, b))
                    dve.wait_ge(y_read.sem, y_read.after(t, 4 + b))
                    for half in range(b in Y_POOL, 2):
                        y = q_gate[:, 2 * b + half, :]
                        dve.scalar_tensor_tensor(y, y, y_scale[:, b:b + 1], x_in[:, 2 * b + half, :], ALU.mult, ALU.add).then_inc(finished.sem, 1)
            assert links[0] == dve_step.per_tile, links[0]

        @block.gpsimd
        def _(pool):
            for c in (lo_split, k_dec_done, k_chunk_end, k_end_done, p_normed, mixa_lo, mixh_lo, x_added,
                      y_scaled, finished_pool):
                c.start(pool)
            def split_lo(tile, w):
                pool.wait_ge(hi_split.sem, hi_split.after(tile, w))
                s = SPLIT_SLOT[w]
                pool.tensor_tensor(w_lo[:, s, :, :], w_raw[:, RAW_SLOT[w], :, :], w_hi[:, s, :, :], ALU.subtract).then_inc(lo_split.sem, 1)

            def norm_probs(t, c):
                pr = probs[:, c % 2, :, :]
                pool.wait_ge(p_inv.sem, p_inv.after(t, c))
                pool.tensor_tensor(pr, pr, s_inv[:, :].unsqueeze(2).broadcast_to([P, 4, P]), ALU.mult).then_inc(p_normed.sem, 1)

            def add_x(tile, k):
                pool.wait_ge(x_squared.sem, x_squared.after(tile, k))
                pool.wait_ge(x_added.sem, x_added.after(tile, k - 2))
                pool.tensor_tensor(x_acc[:, :], x_acc[:, :], x_sq[:, :], ALU.add).then_inc(x_added.sem, 1)

            pool.wait_ge(lo_split.sem, lo_split.after(0, 0))
            split_lo(0, 1)
            for i in range(1, FIRST_POOL):
                pool.wait_ge(x_squared.sem, x_squared.after(0, i))
                if i > 1:
                    pool.wait_ge(pool_sum, i - 1)
                pool.tensor_tensor(x_sq[:, :], x_sq[:, :] if i > 1 else q_gate[:, FIRST_SQUARES[0], :],
                                   q_gate[:, FIRST_SQUARES[i], :], ALU.add).then_inc(pool_sum, 1)
            with pool.Fori(0, TILES) as t:
                for s in range(WT):
                    g, c = s - PAIR0, s - SCORES0
                    h_of, kind = divmod(s - 1 - H0, 4) if H0 < s <= OUT0 else (0, None)
                    if kind == 2:
                        pool.wait_ge(f_exp.sem, f_exp.after(t, h_of))
                        pool.wait_ge(a_u.sem, a_u.after(t, PAIRS * h_of - 1))
                        pool.tensor_tensor(k_dec[:, :], f_a[:, :], f_b[:, :], ALU.mult).then_inc(k_dec_done.sem, 1)
                    if s - 1 in XSQ[1:]:
                        add_x(t + 1, XSQ.index(s - 1))
                    for j in MIXA.get(s - 1, ()):
                        pool.wait_ge(mixa_hi.sem, mixa_hi.after(t, j))
                        pool.tensor_tensor(mix_lo[:, j, :], q_gate[:, QT + j, :], mix_hi[:, j, :], ALU.subtract).then_inc(mixa_lo.sem, 1)
                    if 1 <= g < G and g % PAIRS == 0:
                        h = g // PAIRS - 1
                        pool.wait_ge(mixh_hi.sem, mixh_hi.after(t, h))
                        pool.tensor_tensor(mix_lo[:, QT + h, :], h_mix[:, :], mix_hi[:, QT + h, :],
                                           ALU.subtract).then_inc(mixh_lo.sem, 1)
                    if 0 <= c < 3:
                        norm_probs(t, c)
                    for w in split_at(s):
                        split_lo(t + w // WT, w % WT)
                    if kind == 1:
                        pool.wait_ge(f_end.sem, f_end.after(t, h_of))
                        pool.wait_ge(a_u.sem, a_u.after(t, PAIRS * h_of - 1))
                        pool.tensor_tensor(k_end[:, :, 0::2, :], by_pair(f_a[:, :]), by_pair(f_c[:, :]), ALU.mult).then_inc(k_chunk_end.sem, 1)
                    if 3 <= c < CHUNKS:
                        norm_probs(t, c)
                    if kind == 1:
                        pool.wait_ge(k_chunk_end.sem, k_chunk_end.after(t, h_of))
                        pool.tensor_tensor(k_end[:, :, 1, :], k_end[:, :, 0, :], decays(h_of, 1), ALU.mult).then_inc(k_end_done.sem, 1)
                pool.wait_ge(y_read.sem, y_read.after(t, 3))
                pool.wait_ge(res_loaded, t * 32 + 32)
                for b in Y_POOL:
                    y = q_gate[:, 2 * b, :]
                    pool.wait_ge(y_rstd.sem, y_rstd.after(t, b))
                    pool.tensor_tensor(y, y, y_scale[:, b:b + 1].broadcast_to([P, N]), ALU.mult).then_inc(y_scaled.sem, 1)
                    pool.wait_ge(y_scaled.sem, y_scaled.after(t, b // 2))
                    pool.tensor_tensor(y, y, x_in[:, 2 * b, :], ALU.add).then_inc(finished_pool.sem, 1)


def weight_tiles(w_in, w_out):
    head = lambda start, j: slice(start + 64 * j, start + 64 * j + 64)
    starts = np.cumsum([0, 512, 128, 128, 512, 512, 512, 512])
    q_a, k_a, v_a, z_a, q_r, f_r, i_r, z_r = (int(v) for v in starts)
    columns = [w_in[:, k_a:k_a + P], w_in[:, v_a:v_a + P]]
    for start in (q_a, z_a):
        columns += [w_in[:, head(start, j + QT * g)] for j in range(QT) for g in range(2)]
    for h in range(HEADS):
        columns += [w_in[:, start + P * h:start + P * (h + 1)] for start in (f_r, q_r, i_r, z_r)]
    columns = np.concatenate(columns, axis=1).reshape(KT, P, OUT0, P).transpose(2, 1, 0, 3)
    rows = [w_out[head(0, j + QT * g)] for j in range(QT) for g in range(2)] + [w_out[512:]]
    rows = np.concatenate(rows, axis=0).reshape(4, 2, P, 2, N).transpose(3, 0, 2, 1, 4)
    return np.concatenate([columns.reshape(OUT0 * P, KT * P), rows.reshape(KT * P, KT * P)], axis=0)


def rope_tables():
    half = 32
    inv = np.float32(ROPE_THETA) ** (-np.arange(half, dtype=np.float32) / np.float32(half))
    angle = inv[:, None] * np.arange(SEQ, dtype=np.float32)[None, :]
    cos, sin = np.cos(angle), np.sin(angle)
    cos, sin = np.concatenate([cos] * 4, axis=0), np.concatenate([-sin, sin, -sin, sin], axis=0)
    tiled = lambda a: np.ascontiguousarray(a.reshape(P, TILES, N).transpose(1, 0, 2).reshape(TILES * P, N), dtype=np.float32)
    return tiled(cos), tiled(sin)


def kernel(x, w_norm_pre, w_in, attn_sinks, hgrn_lb, hgrn_norm, w_out, w_norm_post):
    import concourse.bacc as bacc
    from concourse.bass_utils import run_bass_kernel_spmd

    x = np.asarray(x)
    by_tile = x[0].reshape(TILES, N, KT, P).transpose(0, 3, 2, 1).reshape(TILES * P, KT * N)
    cos, sin = rope_tables()
    by_partition = lambda v: np.asarray(v).reshape(-1, P).T
    sinks = np.repeat(np.asarray(attn_sinks)[0].reshape(2, 2, 2).transpose(2, 0, 1).reshape(2, 4), CHUNK, axis=0)
    vectors = np.concatenate([by_partition(w_norm_pre), by_partition(hgrn_norm),
                              by_partition(hgrn_lb), sinks], axis=1)
    m, l = np.arange(P)[:, None], np.arange(P)[None, :]
    squares = np.concatenate([np.eye(P), l >= m], axis=1).astype(np.float32)
    arrays = {
        "x": by_tile, "x_rows": x[0], "weights": weight_tiles(np.asarray(w_in)[0], np.asarray(w_out)[0]),
        "cos": cos, "sin": sin, "vectors": vectors,
        "w_post": np.broadcast_to(np.asarray(w_norm_post), (P, D_MODEL)), "squares": squares,
    }
    arrays = {f"in_{name}": np.ascontiguousarray(a) for name, a in arrays.items()}

    nc = bacc.Bacc("TRN2", target_bir_lowering=False, num_devices=1)
    aps = [nc.dram_tensor(name, a.shape, FP32, kind="ExternalInput").ap() for name, a in arrays.items()]
    out = nc.dram_tensor("out", (SEQ, D_MODEL), FP32, kind="ExternalOutput").ap()
    hybrid_block(nc, *aps, out)
    got = run_bass_kernel_spmd(nc, [arrays], core_ids=[0]).results[0]["out"]
    return got.reshape(1, SEQ, D_MODEL)
```
